# Optimizing a Trainium2 kernel written in Bass

```python
import jax, jax.numpy as jnp
from jax import lax
import numpy as np

D_MODEL = 1024
BATCH = 1
SEQ = 1024
DEPTH = 1

CHUNK = 64
Q_BLOCK = 128
ATT_HEADS = 16
HEAD_DIM = 64
D_ATT = ATT_HEADS * HEAD_DIM
D_RNN = D_MODEL
RNN_BLOCKS = 16
RNN_BLOCK_W = D_RNN // RNN_BLOCKS
CONV_W = 4
RG_C = 8.0
NORM_EPS = 1e-6
MASK_VALUE = -1e30
IN_WIDTHS = (D_ATT, D_ATT, D_ATT, ATT_HEADS, D_ATT, D_RNN, D_RNN, D_MODEL, D_MODEL)
IN_TOTAL = 5 * D_ATT + ATT_HEADS + 2 * D_RNN + 2 * D_MODEL

kernel_name = "hybrid_fox_rglru_gated_block"

def rms_norm(x, w):
    xf = x.astype(jnp.float32)
    y = xf * lax.rsqrt(jnp.mean(xf * xf, axis=-1, keepdims=True) + NORM_EPS)
    return (y * w.astype(jnp.float32)).astype(x.dtype)

def split_columns(z):
    parts = []
    start = 0
    for width in IN_WIDTHS:
        parts.append(z[..., start:start + width])
        start += width
    return parts

def forgetting_attention(q, k, v, log_f):
    seq = q.shape[1]
    scale = HEAD_DIM ** -0.5
    c = jnp.transpose(jnp.cumsum(log_f, axis=1), (0, 2, 1))
    outs = []
    for blk in range(seq // Q_BLOCK):
        q0 = blk * Q_BLOCK
        q1 = q0 + Q_BLOCK
        qb = q[:, q0:q1]
        kb = k[:, :q1]
        vb = v[:, :q1]
        s = jnp.einsum('bqhd,bkhd->bhqk', qb, kb).astype(jnp.float32) * scale
        s = s + c[:, :, q0:q1][:, :, :, None] - c[:, :, :q1][:, :, None, :]
        mask = (q0 + jnp.arange(Q_BLOCK))[:, None] >= jnp.arange(q1)[None, :]
        s = jnp.where(mask[None, None], s, MASK_VALUE)
        p = jax.nn.softmax(s, axis=-1)
        outs.append(jnp.einsum('bhqk,bkhd->bqhd', p.astype(vb.dtype), vb))
    return jnp.concatenate(outs, axis=1)

def causal_depthwise_conv(x, w, b):
    seq = x.shape[1]
    xp = jnp.pad(x, ((0, 0), (CONV_W - 1, 0), (0, 0)))
    y = b + w[0] * xp[:, 0:seq]
    for j in range(1, CONV_W):
        y = y + w[j] * xp[:, j:j + seq]
    return y

def rg_lru(x, r, i, lam):
    log_a = -RG_C * r.astype(jnp.float32) * jax.nn.softplus(-lam.astype(jnp.float32))
    a = jnp.exp(log_a)
    u = jnp.sqrt(jnp.maximum(-jnp.expm1(2.0 * log_a), 0.0)) * (
        i.astype(jnp.float32) * x.astype(jnp.float32))
    a_t = jnp.swapaxes(a, 0, 1)
    u_t = jnp.swapaxes(u, 0, 1)

    def step(h, inp):
        a_s, u_s = inp
        h = a_s * h + u_s
        return h, h

    h0 = jnp.zeros(a_t.shape[1:], jnp.float32)
    _, hs = lax.scan(step, h0, (a_t, u_t))
    return jnp.swapaxes(hs, 0, 1).astype(x.dtype)

def setup_inputs(seed: int = 0) -> dict:
    key = jax.random.key(seed)
    ks = jax.random.split(key, 18)
    f32 = jnp.float32
    L = DEPTH

    def nrm(k, shape, fan_in):
        return jax.random.normal(k, shape, f32) * (fan_in ** -0.5)

    x = jax.random.normal(ks[0], (BATCH, SEQ, D_MODEL), f32)
    pre_norm_w = 1.0 + 0.05 * jax.random.normal(ks[1], (L, D_MODEL), f32)
    w_in = nrm(ks[2], (L, D_MODEL, IN_TOTAL), D_MODEL)
    b_in = 0.02 * jax.random.normal(ks[3], (L, IN_TOTAL), f32)
    conv_w = nrm(ks[4], (L, CONV_W, D_RNN), CONV_W)
    conv_b = 0.02 * jax.random.normal(ks[5], (L, D_RNN), f32)
    rg_wa = nrm(ks[6], (L, RNN_BLOCKS, RNN_BLOCK_W, RNN_BLOCK_W), RNN_BLOCK_W)
    rg_ba = 0.02 * jax.random.normal(ks[7], (L, D_RNN), f32)
    rg_wx = nrm(ks[8], (L, RNN_BLOCKS, RNN_BLOCK_W, RNN_BLOCK_W), RNN_BLOCK_W)
    rg_bx = 0.02 * jax.random.normal(ks[9], (L, D_RNN), f32)
    u = jax.random.uniform(ks[10], (L, D_RNN), f32, minval=0.9, maxval=0.999)
    a0 = u ** (1.0 / RG_C)
    rg_lambda = jnp.log(a0) - jnp.log1p(-a0)
    w_branch_a = nrm(ks[11], (L, D_ATT, D_MODEL), D_ATT)
    w_branch_r = nrm(ks[12], (L, D_RNN, D_MODEL), D_RNN)
    w_out = nrm(ks[13], (L, D_MODEL, D_MODEL), D_MODEL)
    post_norm_w = 1.0 + 0.05 * jax.random.normal(ks[14], (L, D_MODEL), f32)
    return {"x": x, "pre_norm_w": pre_norm_w, "w_in": w_in, "b_in": b_in,
            "conv_w": conv_w, "conv_b": conv_b, "rg_wa": rg_wa, "rg_ba": rg_ba,
            "rg_wx": rg_wx, "rg_bx": rg_bx, "rg_lambda": rg_lambda,
            "w_branch_a": w_branch_a, "w_branch_r": w_branch_r, "w_out": w_out,
            "post_norm_w": post_norm_w}

def reference(x, pre_norm_w, w_in, b_in, conv_w, conv_b, rg_wa, rg_ba, rg_wx, rg_bx,
              rg_lambda, w_branch_a, w_branch_r, w_out, post_norm_w):
    bsz, seq, _ = x.shape
    for l in range(DEPTH):
        h = rms_norm(x, pre_norm_w[l])
        z = jnp.einsum('bsd,de->bse', h, w_in[l]) + b_in[l]
        q, k, v, f_logit, gate_a, x_r, gate_r, mg_a, mg_r = split_columns(z)

        q = q.reshape(bsz, seq, ATT_HEADS, HEAD_DIM)
        k = k.reshape(bsz, seq, ATT_HEADS, HEAD_DIM)
        v = v.reshape(bsz, seq, ATT_HEADS, HEAD_DIM)
        log_f = jax.nn.log_sigmoid(f_logit.astype(jnp.float32))
        y_a = forgetting_attention(q, k, v, log_f).reshape(bsz, seq, D_ATT)
        y_a = jnp.einsum('bsc,cd->bsd', y_a * jax.nn.silu(gate_a), w_branch_a[l])

        xc = causal_depthwise_conv(x_r, conv_w[l], conv_b[l])
        xb = xc.reshape(bsz, seq, RNN_BLOCKS, RNN_BLOCK_W)
        r = jax.nn.sigmoid(jnp.einsum('bsgi,gij->bsgj', xb, rg_wa[l]).reshape(bsz, seq, D_RNN) + rg_ba[l])
        i = jax.nn.sigmoid(jnp.einsum('bsgi,gij->bsgj', xb, rg_wx[l]).reshape(bsz, seq, D_RNN) + rg_bx[l])
        y_r = rg_lru(xc, r, i, rg_lambda[l])
        y_r = jnp.einsum('bsc,cd->bsd', y_r * jax.nn.silu(gate_r), w_branch_r[l])

        m = jax.nn.sigmoid(mg_a) * y_a + jax.nn.sigmoid(mg_r) * y_r
        o = jnp.einsum('bsd,de->bse', m, w_out[l])
        x = x + rms_norm(o, post_norm_w[l])
    return x


_drawn_inputs = setup_inputs


def setup_inputs(seed=0):
    import zlib

    import numpy as np

    out = dict(_drawn_inputs(seed))
    spreads = {}
    factors = {'rg_ba': 23.228, 'rg_bx': 8.0}
    for name, (base, spread) in spreads.items():
        noise = np.random.default_rng([zlib.crc32(name.encode()), seed]).standard_normal(out[name].shape)
        drawn = base * np.exp(spread * noise) if base else spread * noise
        out[name] = __import__('jax').numpy.asarray(drawn.astype(out[name].dtype))
    for name, factor in factors.items():
        out[name] = (out[name] * factor).astype(out[name].dtype)
    return out
```

```python
import concourse.bass as bass
from concourse import mybir
from contextlib import ExitStack

P = 128
D = 1024
SEQ = 1024
KT = D // P
TT = SEQ // P
CT = D // P
HD = 64
HEADS = D // HD
QB = SEQ // P
UNITS = 2 * QB
BANK = 512
EPS = 1e-6
RG_C = 8.0
MASK = -1e30
SCALE = HD ** -0.5

Q_COL, K_COL, V_COL, F_COL = 0, D, 2 * D, 3 * D
GA_COL = 3 * D + HEADS
XR_COL, GR_COL, MA_COL, MR_COL = (GA_COL + n * D for n in (1, 2, 3, 4))
JOB_COLS = [Q_COL, K_COL, V_COL, XR_COL, GA_COL, GR_COL, MA_COL, MR_COL]
J_Q, J_K, J_V, J_XR, J_GA, J_GR, J_MA, J_MR = range(8)
JOBS = 8
B_Q, B_K, B_V, B_GA, B_XR, B_GR, B_MA, B_MR = range(8)
C_TAP, C_CB, C_BA, C_BX, C_LAM, C_PRE = 0, 4, 5, 6, 7, 8

MM = 6 * KT
A_Q, A_V, A_VT, A_R, A_I, A_MR, FILLS_A = 1, 2, 3, 4, 5, 6, 6
B_FILL_K, B_FILL_XR, B_FILL_GA, B_FILL_GR, B_FILL_MA, FILLS_B = 1, 2, 3, 4, 5, 5
CHUNKS = 2 * sum(1 + (b >= 4) for b in range(QB))
STEPS = UNITS + 2


def chunks_before(u):
    return sum(1 + (v % QB >= 4) for v in range(u))


def filler_plan():
    seq = []
    for name, count, weight in (("GA", MM, 1), ("R", 2, 4), ("GR", MM, 1), ("I", 2, 4), ("MA", MM, 1), ("MR", MM, 1)):
        seq += [(name, n, weight) for n in range(count)]
    total = sum(w for _, _, w in seq)
    plan, read, done, at = [], {}, 0, 0
    for s in range(2 * STEPS):
        part = []
        while at < len(seq) and done < total * (s + 1) / (2 * STEPS):
            part.append(seq[at][:2])
            read[seq[at][0]] = (s + 1) // 2
            done += seq[at][2]
            at += 1
        plan.append(part)
    return plan, read


PLAN, READ = filler_plan()


def build(nc, x, pre_w, w_in, b_in, conv_w, conv_b, rg_wa, rg_ba, rg_wx, rg_bx, lam, w_a, w_r,
          w_out, post_w, out):
    f32, f32r, bf16 = mybir.dt.float32, mybir.dt.float32r, mybir.dt.bfloat16
    ACT, ALU = mybir.ActivationFunctionType, mybir.AluOpType

    w_in_v = w_in[0].rearrange("(k p) c -> p k c", p=P)
    w_a_v = w_a[0].rearrange("(k p) c -> p k c", p=P)
    w_r_v = w_r[0].rearrange("(k p) c -> p k c", p=P)
    w_out_v = w_out[0].rearrange("(k p) c -> k p c", p=P)
    x_v = x[0].rearrange("(t p) d -> t p d", p=P)
    out_v = out[0].rearrange("(t p) d -> t p d", p=P)

    ua_hi_d, ua_lo_d, ur_hi_d, ur_lo_d = (
        nc.dram_tensor(f"{n}_scratch", (CT, P, SEQ), f32, kind="Internal").ap()
        for n in ("ua_hi", "ua_lo", "ur_hi", "ur_lo"))
    sa_d, sr_d = (nc.dram_tensor(f"{n}_scratch", (CT, P, SEQ), f32, kind="Internal").ap()
                  for n in ("sig_a", "sig_r"))
    c_d = nc.dram_tensor("c_scratch", (HEADS, SEQ), f32, kind="Internal").ap()

    ctx = ExitStack()
    with ctx:
        def sb(name, shape, dt=f32, stack=ctx):
            return stack.enter_context(nc.sbuf_tensor(name, shape, dt))

        def sem(name):
            return ctx.enter_context(nc.semaphore(name))

        r1_hi = sb("r1_hi", [P, KT, SEQ], f32r)
        r1_lo = sb("r1_lo", [P, KT, SEQ], f32r)
        raw = sb("raw", [P, 2, KT * P])
        w_hi = sb("w_hi", [P, 2, KT, P], f32r)
        w_lo = sb("w_lo", [P, 2, KT, P], f32r)
        ident = sb("ident", [P, P])
        ident_b = sb("ident_b", [P, P], bf16)
        mask_b = sb("mask_b", [P, P], bf16)
        prm_b = sb("prm_b", [P, 8, CT])
        prm_c = sb("prm_c", [P, 9, CT])
        rgk = sb("rgk", [P, 2, CT])

        ps_a = ctx.enter_context(nc.psum_tensor("ps_a", [P, 2 * BANK], f32))
        ps_b = ctx.enter_context(nc.psum_tensor("ps_b", [P, 2 * BANK], f32))
        ps_s = ctx.enter_context(nc.psum_tensor("ps_s", [P, 2 * BANK], f32))
        ps_t = ctx.enter_context(nc.psum_tensor("ps_t", [P, BANK], f32))
        ps_o = ctx.enter_context(nc.psum_tensor("ps_o", [P, BANK], f32))
        pair = [ps_a, ps_b]

        raw_in = [sem("raw_in_even"), sem("raw_in_odd")]
        s_whi, s_wlo = sem("w_hi_ready"), sem("w_lo_ready")
        s_carry, s_carry_v = sem("wait_carrier_pool"), sem("wait_carrier_vector")
        s_const, s_prm_in, s_prm_t, s_prm = sem("consts"), sem("params_in"), sem("params_t"), sem("params")
        s_x = [sem("x_in_even"), sem("x_in_odd")]
        s_ss, s_std, s_rstd, s_xn = sem("sumsq"), sem("std"), sem("rstd"), sem("x_scaled")
        s_xt, s_hw, s_hhi, s_hlo = sem("x_transposed"), sem("h_weighted"), sem("h_hi"), sem("h_lo")
        s_pro = sem("dve_prologue_step")
        s_wf_in, s_wf, s_f, s_fact, s_c, s_c_out = (sem(n) for n in (
            "wf_in", "wf_split", "f_summed", "f_act", "c_ready", "c_stored"))
        s_sp = sem("softplus_act")
        a_full, b_full = sem("pair_a_full"), sem("pair_b_full")
        s_qhi, s_qlo, s_khi, s_klo, s_kdup, s_v, s_vhi, s_vlo = (sem(n) for n in (
            "q_hi", "q_lo", "k_hi", "k_lo", "k_dup", "v_sb", "v_hi", "v_lo"))
        s_s, s_max, s_neg, s_exp = sem("scores_ready"), sem("row_max"), sem("neg_max"), sem("exp_done")
        s_rinv, s_norm = sem("row_sum_inv"), sem("probs_ready")
        s_t, s_phi, s_plo = sem("probs_t"), sem("p_hi"), sem("p_lo")
        s_pv, s_pvc, s_pva = sem("values_ready"), sem("values_half"), sem("values_added")
        s_cb = sem("c_broadcast_in")
        s_xr, s_conv, s_gw = sem("xr_padded"), sem("conv_step"), sem("gate_weights_in")
        s_ri, s_tanh, s_sq, s_a = sem("r_i_ready"), sem("tanh_ready"), sem("sqrt_ready"), sem("decay_ready")
        s_ix, s_rg, s_gr, s_ur, s_ga, s_ua = (sem(n) for n in (
            "i_times_x", "rg_step", "gate_r_ready", "ur_ready", "gate_a_ready", "ua_ready"))
        s_uhi, s_ulo, s_uout = sem("u_hi"), sem("u_lo"), sem("u_stored")
        s_sig, s_sigout = sem("merge_gate_ready"), sem("merge_gate_stored")
        s_stored = sem("iteration_stored")

        one = ExitStack()
        pt_hi = sb("pt_hi", [P, QB, 2 * P], f32r, one)
        pt_lo = sb("pt_lo", [P, QB, 2 * P], f32r, one)
        q_st = sb("q_st", [P, 2, SEQ], f32r, one)
        k_hi = sb("k_hi", [P, 2, SEQ], f32r, one)
        k_lo = sb("k_lo", [P, 2, SEQ], f32r, one)
        v_st = sb("v_st", [P, QB, 2, P], f32r, one)
        probs = sb("probs", [P, 3, SEQ], f32, one)
        cb = sb("cb", [P, 2, SEQ], f32, one)
        stage = sb("stage", [P, SEQ], f32, one)
        gate_a = sb("gate_a", [P, SEQ], f32, one)
        y_t = sb("y_t", [P, SEQ], f32, one)
        half = sb("half", [P, 2 * P], f32, one)
        u_hi = sb("u_hi", [P, SEQ], f32r, one)
        u_lo = sb("u_lo", [P, SEQ], f32r, one)
        PAD = 3
        xpad = sb("xpad", [P, PAD + SEQ], f32, one)
        xc = sb("xc", [P, SEQ], f32, one)
        r_t = sb("r_t", [P, SEQ], f32, one)
        i_t = sb("i_t", [P, SEQ], f32, one)
        a_t = sb("a_t", [P, SEQ], f32, one)
        s_tl = sb("s_tl", [P, SEQ], f32, one)
        gw = sb("gw", [P, 2, P], f32, one)
        mx = sb("mx", [P, UNITS], f32, one)
        ngm = sb("ngm", [P, UNITS], f32, one)
        rs = sb("rs", [P, UNITS], f32, one)
        rinv = sb("rinv", [P, UNITS], f32, one)
        st8 = sb("st8", [P, 4, TT], f32, one)
        wf_raw = sb("wf_raw", [P, KT, HEADS], f32, one)
        wf = sb("wf", [P, KT, 3 * HEADS], f32r, one)
        bf = sb("bf", [HEADS, 1], f32, one)
        sp = sb("sp", [P, 5, CT], f32, one)
        prm_in = sb("prm_in", [72, P], f32, one)
        prm_in_b = sb("prm_in_b", [64, P], f32, one)
        f_lo, f_a, f_b, f_l, f_c = (z[0:HEADS, :] for z in (xc, i_t, a_t, s_tl, r_t))
        ones_f = y_t[0:HEADS, :]

        def project(pe, slot, dst, first, last):
            for n in range(first, last):
                kt, part = divmod(n, 6)
                w = (w_hi if part < 4 else w_lo)[:, slot, kt, :]
                h = r1_lo if part in (2, 3) else r1_hi
                b = part % 2
                mm = nc.tensor.matmul(dst[:, b * BANK:(b + 1) * BANK], w,
                                      h[:, kt, b * BANK:(b + 1) * BANK],
                                      start=(kt == 0 and part < 2), stop=(kt == KT - 1 and part >= 4))
            return mm

        with nc.Block() as block:

            @block.sync
            def _(sp_):
                for s in (s_max, s_stored, s_sig, s_ur, s_ri, s_pva, s_plo):
                    sp_.sem_inc(s, 1)
                sp_.sem_inc(s_wlo, 2)
                sp_.dma_start(prm_in_b[0:24, :], b_in[0, 0:3 * D].rearrange("(r c) -> r c", c=P)).then_inc(s_prm_in, 16)
                sp_.dma_start(prm_in_b[24:64, :], b_in[0, GA_COL:GA_COL + 5 * D].rearrange("(r c) -> r c", c=P)).then_inc(s_prm_in, 16)
                sp_.dma_start(prm_in[0:32, :], conv_w[0].rearrange("j (r c) -> (j r) c", c=P)).then_inc(s_prm_in, 16)
                for n, v in enumerate((conv_b, rg_ba, rg_bx, lam, pre_w)):
                    sp_.dma_start(prm_in[32 + 8 * n:40 + 8 * n, :], v[0].rearrange("(r c) -> r c", c=P)).then_inc(s_prm_in, 16)
                for t in range(2):
                    sp_.dma_start(probs[:, t, :], x_v[t]).then_inc(s_x[t], 16)
                sp_.dma_start(wf_raw[:, :, :], w_in_v[:, :, F_COL:F_COL + HEADS]).then_inc(s_wf_in, 16)
                sp_.dma_start(bf[:, :], b_in[0, F_COL:F_COL + HEADS].rearrange("(h o) -> h o", o=1)).then_inc(s_wf_in, 16)
                with sp_.Fori(0, CT) as i:
                    for r in range(JOBS):
                        sp_.wait_ge(s_wlo, i * JOBS + (r + 1))
                        sp_.dma_start(raw[:, r % 2, :].rearrange("p (k c) -> p k c", c=P),
                                      w_in_v[:, :, bass.ds(i * P + JOB_COLS[r], P)]).then_inc(raw_in[r % 2], 16)

                for r in range(2):
                    sp_.wait_ge(s_wlo, CT * JOBS + (r + 1))
                    sp_.dma_start(raw[:, r, :].rearrange("p (k c) -> p k c", c=P),
                                  w_a_v[:, :, r * P:(r + 1) * P]).then_inc(raw_in[r], 16)

            @block.gpsimd
            def _(pool):
                nc.gpsimd.memset(ident[:, :], 0.0).then_inc(s_const, 1)
                nc.gpsimd.memset(ident_b[:, :], 0.0).then_inc(s_const, 1)
                nc.gpsimd.memset(mask_b[:, :], 0.0).then_inc(s_const, 1)
                pool.wait_ge(s_const, 3)
                for m in (ident, ident_b):
                    nc.gpsimd.affine_select(out=m[:, :], in_=m[:, :], compare_op=ALU.not_equal, fill=1.0,
                                            base=0, pattern=[[-1, P]], channel_multiplier=1).then_inc(s_const, 1)
                nc.gpsimd.affine_select(out=mask_b[:, :], in_=mask_b[:, :], compare_op=ALU.is_ge, fill=MASK,
                                        base=0, pattern=[[-1, P]], channel_multiplier=1).then_inc(s_const, 1)
                nc.gpsimd.memset(gw[:, :, :], 0.0).then_inc(s_const, 1)
                nc.gpsimd.memset(xpad[:, 0:PAD], 0.0).then_inc(s_const, 1)
                pool.wait_ge(s_const, 8)
                pool.wait_ge(s_c, 1)
                pool.dma_start(c_d, f_c).then_inc(s_c_out, 16)
                pool.wait_ge(s_c_out, 16)
                with pool.Fori(0, CT) as i:
                    pool.wait_ge(s_max, i * UNITS + 1)
                    pool.sem_inc(s_carry, 1)
                    for h in range(2):
                        pool.dma_start(cb[:, h, :], c_d[bass.ds(i * 2 + h, 1), :].to_broadcast([P, SEQ])).then_inc(s_cb, 16)
                    pool.wait_ge(s_ri, i * 2 + 1)
                    pool.sem_inc(s_carry, 1)
                    for g, w in enumerate((rg_wa, rg_wx)):
                        for b in range(2):
                            pool.dma_start(gw[b * HD:(b + 1) * HD, g, b * HD:(b + 1) * HD],
                                           w[0, bass.ds(i * 2 + b, 1), :, :].rearrange("o a b -> (o a) b")).then_inc(s_gw, 16)
                    pool.wait_ge(s_klo, i * 2 + 2)
                    pool.sem_inc(s_carry, 1)
                    for t in (k_hi, k_lo):
                        pool.dma_start(t[HD:P, 0, :].bitcast(f32), t[0:HD, 0, :].bitcast(f32)).then_inc(s_kdup, 16)
                        pool.dma_start(t[0:HD, 1, :].bitcast(f32), t[HD:P, 1, :].bitcast(f32)).then_inc(s_kdup, 16)
                    pool.wait_ge(s_ri, i * 2 + 3)
                    pool.wait_ge(s_conv, i * 4 + 4)
                    nc.gpsimd.tensor_tensor(i_t[:, :], i_t[:, :], xc[:, :], ALU.mult).then_inc(s_ix, 1)
                    pool.wait_ge(s_gr, i + 1)
                    pool.wait_ge(s_rg, i * 3 + 3)
                    nc.gpsimd.tensor_tensor(r_t[:, :], r_t[:, :], xpad[:, PAD:], ALU.mult).then_inc(s_ur, 1)
                    pool.wait_ge(s_ulo, i * 2 + 1)
                    pool.sem_inc(s_carry, 1)
                    pool.dma_start(ur_hi_d[bass.ds(i, 1)].rearrange("o p c -> (o p) c"), u_hi[:, :].bitcast(f32)).then_inc(s_uout, 16)
                    pool.dma_start(ur_lo_d[bass.ds(i, 1)].rearrange("o p c -> (o p) c"), u_lo[:, :].bitcast(f32)).then_inc(s_uout, 16)
                    pool.wait_ge(s_sig, i * 2 + 2)
                    pool.sem_inc(s_carry, 1)
                    pool.dma_start(sa_d[bass.ds(i, 1)].rearrange("o p c -> (o p) c"), stage[:, :]).then_inc(s_sigout, 16)
                    pool.wait_ge(s_sig, i * 2 + 3)
                    pool.sem_inc(s_carry, 1)
                    pool.dma_start(sr_d[bass.ds(i, 1)].rearrange("o p c -> (o p) c"), stage[:, :]).then_inc(s_sigout, 16)
                    pool.wait_ge(s_pva, i * QB + (QB + 1))
                    pool.wait_ge(s_ga, i + 1)
                    pool.wait_ge(s_uout, i * 64 + 32)
                    nc.gpsimd.tensor_tensor(y_t[:, :], y_t[:, :], gate_a[:, :], ALU.mult).then_inc(s_ua, 1)
                    pool.wait_ge(s_ulo, i * 2 + 2)
                    pool.sem_inc(s_carry, 1)
                    pool.dma_start(ua_hi_d[bass.ds(i, 1)].rearrange("o p c -> (o p) c"), u_hi[:, :].bitcast(f32)).then_inc(s_uout, 16)
                    pool.dma_start(ua_lo_d[bass.ds(i, 1)].rearrange("o p c -> (o p) c"), u_lo[:, :].bitcast(f32)).then_inc(s_uout, 16)
                    pool.wait_ge(s_uout, i * 64 + 64)
                    pool.wait_ge(s_sigout, i * 32 + 32)
                    pool.sem_inc(s_stored, 1)

            @block.scalar
            def _(act):
                act.wait_ge(s_prm, 2)
                act.wait_ge(s_pro, 3)
                nc.scalar.activation(sp[:, 0, :], sp[:, 1, :], ACT.Exp, scale=-1.0).then_inc(s_sp, 1)
                for t in range(TT):
                    act.wait_ge(s_x[t % 2], 16 * (t // 2 + 1))
                    nc.scalar.activation(gate_a[:, :], probs[:, t % 2, :], ACT.Square,
                                         accum_out=st8[:, 0, t:t + 1]).then_inc(s_ss, 1)
                    act.wait_ge(s_ss, 2 * t + 2)
                    nc.scalar.activation(st8[:, 2, t:t + 1], st8[:, 1, t:t + 1], ACT.Sqrt).then_inc(s_std, 1)
                    act.wait_ge(s_rstd, t + 1)
                    nc.scalar.activation(probs[:, t % 2, :], probs[:, t % 2, :], ACT.Identity,
                                         scale=st8[:, 3, t:t + 1]).then_inc(s_xn, 1)
                    act.wait_ge(s_hw, t + 1)
                    nc.scalar.activation(r1_hi[:, :, t * P:(t + 1) * P],
                                         stage[:, :].rearrange("p (k c) -> p k c", c=P), ACT.Copy).then_inc(s_hhi, 1)
                    if t + 2 < TT:
                        act.dma_start(probs[:, t % 2, :], x_v[t + 2]).then_inc(s_x[t % 2], 16)
                act.wait_ge(s_wf_in, 32)
                act.wait_ge(s_wf, 1)
                nc.scalar.activation(wf[:, :, 0:HEADS], wf_raw[:, :, :], ACT.Copy).then_inc(s_wf, 1)
                for j in range(2):
                    act.wait_ge(raw_in[j], 16)
                    nc.scalar.activation(w_hi[:, j, :, :], raw[:, j, :].rearrange("p (k c) -> p k c", c=P), ACT.Copy).then_inc(s_whi, 1)
                act.wait_ge(a_full, 1)
                nc.scalar.activation(f_lo, ps_a[2 * HEADS:3 * HEADS, :], ACT.Identity).then_inc(s_fact, 1)
                act.wait_ge(s_f, 1)
                nc.scalar.activation(f_b, f_a, ACT.Abs).then_inc(s_fact, 1)
                act.wait_ge(s_fact, 2)
                nc.scalar.activation(f_b, f_b, ACT.Exp, scale=-1.0).then_inc(s_fact, 1)
                act.wait_ge(s_fact, 3)
                nc.scalar.activation(f_l, f_b, ACT.Ln, bias=1.0).then_inc(s_fact, 1)

                with act.Fori(0, CT) as i:

                    def split_hi(r):
                        act.wait_ge(raw_in[r % 2], i * (JOBS * 8) + 16 * (r // 2 + 1))
                        nc.scalar.activation(w_hi[:, r % 2, :, :], raw[:, r % 2, :].rearrange("p (k c) -> p k c", c=P),
                                             ACT.Copy).then_inc(s_whi, 1)

                    bias = lambda row: prm_b[:, row, bass.ds(i, 1)]
                    bias_c = lambda row: prm_c[:, row, bass.ds(i, 1)]
                    act.wait_ge(a_full, i * FILLS_A + (A_Q + 1))
                    for h in range(2):
                        rows = slice(h * HD, (h + 1) * HD)
                        nc.scalar.activation(q_st[rows, h, :], ps_a[rows, :], ACT.Identity,
                                             bias=prm_b[rows, B_Q, bass.ds(i, 1)]).then_inc(s_qhi, 1)
                    split_hi(2)
                    act.wait_ge(b_full, i * FILLS_B + B_FILL_K)
                    for h in range(2):
                        rows = slice(h * HD, (h + 1) * HD)
                        nc.scalar.activation(k_hi[rows, h, :], ps_b[rows, :], ACT.Identity,
                                             bias=prm_b[rows, B_K, bass.ds(i, 1)]).then_inc(s_khi, 1)
                    split_hi(3)
                    act.wait_ge(a_full, i * FILLS_A + (A_V + 1))
                    act.wait_ge(s_stored, i + 1)
                    nc.scalar.activation(stage[:, :], ps_a[:, :], ACT.Identity, bias=bias(B_V)).then_inc(s_v, 1)
                    split_hi(4)
                    act.wait_ge(b_full, i * FILLS_B + B_FILL_XR)
                    act.wait_ge(s_ur, i + 1)
                    nc.scalar.activation(xpad[:, PAD:], ps_b[:, :], ACT.Identity, bias=bias(B_XR)).then_inc(s_xr, 1)
                    act.wait_ge(a_full, i * FILLS_A + (A_VT + 1))
                    nc.scalar.activation(v_st[:, :, :, 0:HD],
                                         ps_a[:, :].rearrange("p (k h c) -> p k h c", h=2, c=HD), ACT.Copy).then_inc(s_vhi, 1)
                    split_hi(5)

                    for s in range(STEPS + 1):
                        if 2 <= s < UNITS + 2:
                            u = s - 2
                            qb = u % QB
                            for c in range(1 + (qb >= 4)):
                                b0, b1 = 4 * c, min(4 * c + 4, qb + 1)
                                act.wait_ge(s_t, i * CHUNKS + (chunks_before(u) + c + 1))
                                nc.scalar.activation(pt_hi[:, b0:b1, (qb % 2) * P:(qb % 2 + 1) * P],
                                                     ps_t[:, 0:(b1 - b0) * P].rearrange("p (b c) -> p b c", c=P),
                                                     ACT.Copy).then_inc(s_phi, 1)
                        if s == READ["GA"]:
                            act.wait_ge(b_full, i * FILLS_B + B_FILL_GA)
                            nc.scalar.activation(gate_a[:, :], ps_b[:, :], ACT.Silu, bias=bias(B_GA)).then_inc(s_ga, 1)
                        if s == READ["GA"] + 1:
                            split_hi(6)
                        if s == READ["R"]:
                            act.wait_ge(a_full, i * FILLS_A + (A_R + 1))
                            nc.scalar.activation(r_t[:, :], ps_a[:, :], ACT.Sigmoid, bias=bias_c(C_BA)).then_inc(s_ri, 1)
                        if s == READ["R"] + 1:
                            act.wait_ge(s_ri, i * 2 + 2)
                            nc.scalar.activation(s_tl[:, :], r_t[:, :], ACT.Tanh, scale=rgk[:, 1, bass.ds(i, 1)]).then_inc(s_tanh, 1)
                            nc.scalar.activation(a_t[:, :], r_t[:, :], ACT.Exp, scale=rgk[:, 0, bass.ds(i, 1)]).then_inc(s_a, 1)
                        if s == READ["R"] + 3:
                            act.wait_ge(s_tanh, i + 1)
                            nc.scalar.activation(s_tl[:, :], s_tl[:, :], ACT.Sqrt).then_inc(s_sq, 1)
                        if s == READ["GR"]:
                            act.wait_ge(b_full, i * FILLS_B + B_FILL_GR)
                            nc.scalar.activation(xpad[:, PAD:], ps_b[:, :], ACT.Silu, bias=bias(B_GR)).then_inc(s_gr, 1)
                        if s == READ["GR"] + 2:
                            split_hi(7)
                        if s == READ["I"]:
                            act.wait_ge(a_full, i * FILLS_A + (A_I + 1))
                            nc.scalar.activation(i_t[:, :], ps_a[:, :], ACT.Sigmoid, bias=bias_c(C_BX)).then_inc(s_ri, 1)
                        if s == READ["I"] + 5:
                            act.wait_ge(s_ur, i + 2)
                            nc.scalar.activation(u_hi[:, :], r_t[:, :], ACT.Copy).then_inc(s_uhi, 1)
                        if s == READ["MA"]:
                            act.wait_ge(b_full, i * FILLS_B + B_FILL_MA)
                            nc.scalar.activation(stage[:, :], ps_b[:, :], ACT.Sigmoid, bias=bias(B_MA)).then_inc(s_sig, 1)
                        if s == READ["MA"] + 1:
                            split_hi(8)
                        if s == READ["MR"]:
                            act.wait_ge(a_full, i * FILLS_A + (A_MR + 1))
                            act.wait_ge(s_sigout, i * 32 + 16)
                            nc.scalar.activation(stage[:, :], ps_a[:, :], ACT.Sigmoid, bias=bias(B_MR)).then_inc(s_sig, 1)
                            split_hi(9)
                        if s < UNITS:
                            n = (s % QB + 1) * P
                            act.wait_ge(s_neg, i * UNITS + (s + 1))
                            nc.scalar.activation(probs[:, s % 3, 0:n], probs[:, s % 3, 0:n], ACT.Exp, scale=SCALE,
                                                 bias=ngm[:, s:s + 1], accum_out=rs[:, s:s + 1]).then_inc(s_exp, 1)
                        if 3 <= s < STEPS and s % 2:
                            g = (s - 3) // 2
                            mine, other = (slice(0, HD), slice(HD, P)) if g < QB // 2 else (slice(HD, P), slice(0, HD))
                            act.wait_ge(s_pv, i * QB + (g + 1))
                            nc.scalar.activation(half[mine, :], ps_o[other, 0:2 * P], ACT.Copy).then_inc(s_pvc, 1)
                    act.wait_ge(s_ua, i + 1)
                    nc.scalar.activation(u_hi[:, :], y_t[:, :], ACT.Copy).then_inc(s_uhi, 1)

            @block.vector
            def _(dve):
                pro = [0]

                def seq(ins):
                    pro[0] += 1
                    ins.then_inc(s_pro, 1)
                    dve.wait_ge(s_pro, pro[0])

                dve.wait_ge(s_prm_t, 1)
                nc.vector.tensor_copy(prm_b[:, :, :], ps_s[:, 0:64].rearrange("p (a b) -> p a b", b=CT)).then_inc(s_prm, 1)
                dve.wait_ge(s_prm_t, 2)
                nc.vector.tensor_copy(prm_c[:, :, :], ps_s[:, BANK:BANK + 72].rearrange("p (a b) -> p a b", b=CT)).then_inc(s_prm, 1)
                dve.wait_ge(s_prm, 2)
                seq(nc.vector.memset(wf[:, :, HEADS:2 * HEADS].bitcast(mybir.dt.uint32), 0))
                seq(nc.vector.tensor_scalar(sp[:, 2, :], prm_c[:, C_LAM, :], -1.0, None, ALU.mult))
                seq(nc.vector.tensor_tensor(sp[:, 1, :], sp[:, 2, :], prm_c[:, C_LAM, :], ALU.max))
                dve.wait_ge(s_sp, 1)
                seq(nc.vector.tensor_scalar(sp[:, 1, :], sp[:, 0, :], 2.0, None, ALU.add))
                seq(nc.vector.reciprocal(sp[:, 3, :], sp[:, 1, :]))
                seq(nc.vector.tensor_tensor(sp[:, 1, :], sp[:, 0, :], sp[:, 3, :], ALU.mult))
                seq(nc.vector.tensor_tensor(sp[:, 3, :], sp[:, 1, :], sp[:, 1, :], ALU.mult))
                seq(nc.vector.tensor_scalar(sp[:, 4, :], sp[:, 3, :], 1.0 / 17, 1.0 / 15, ALU.mult, ALU.add))
                for k in (13, 11, 9, 7, 5, 3, 1):
                    seq(nc.vector.tensor_tensor(sp[:, 4, :], sp[:, 4, :], sp[:, 3, :], ALU.mult))
                    seq(nc.vector.tensor_scalar(sp[:, 4, :], sp[:, 4, :], 1.0 / k, None, ALU.add))
                seq(nc.vector.tensor_tensor(sp[:, 4, :], sp[:, 4, :], sp[:, 1, :], ALU.mult))
                seq(nc.vector.tensor_scalar(sp[:, 2, :], sp[:, 2, :], 0.0, None, ALU.max))
                seq(nc.vector.scalar_tensor_tensor(sp[:, 3, :], sp[:, 4, :], 2.0, sp[:, 2, :], ALU.mult, ALU.add))
                seq(nc.vector.tensor_scalar(rgk[:, 0, :], sp[:, 3, :], -RG_C, None, ALU.mult))
                seq(nc.vector.tensor_scalar(rgk[:, 1, :], sp[:, 3, :], RG_C / 2, None, ALU.mult))

                for t in range(TT):
                    dve.wait_ge(s_ss, 2 * t + 1)
                    nc.vector.tensor_scalar(st8[:, 1, t:t + 1], st8[:, 0, t:t + 1], 1.0 / D, EPS, ALU.mult, ALU.add).then_inc(s_ss, 1)
                    dve.wait_ge(s_std, t + 1)
                    nc.vector.reciprocal(st8[:, 3, t:t + 1], st8[:, 2, t:t + 1]).then_inc(s_rstd, 1)
                    dve.wait_ge(s_xt, t + 1)
                    if t:
                        dve.wait_ge(s_hlo, t)
                    nc.vector.tensor_tensor(stage[:, :].rearrange("p (k c) -> p k c", c=P),
                                            pair[t % 2][:, :].rearrange("p (k c) -> p k c", c=P),
                                            prm_c[:, C_PRE, :].unsqueeze(2).to_broadcast([P, KT, P]), ALU.mult).then_inc(s_hw, 1)
                    dve.wait_ge(s_hhi, t + 1)
                    dve.wait_ge(s_hw, t + 1)
                    nc.vector.tensor_tensor(r1_lo[:, :, t * P:(t + 1) * P],
                                            stage[:, :].rearrange("p (k c) -> p k c", c=P),
                                            r1_hi[:, :, t * P:(t + 1) * P].bitcast(f32), ALU.subtract).then_inc(s_hlo, 1)
                dve.wait_ge(s_wf_in, 32)
                seq(nc.vector.memset(ones_f, 1.0))
                nc.vector.memset(half[:, 0:1], 0.0).then_inc(s_wf, 1)
                dve.wait_ge(s_wf, 2)
                nc.vector.tensor_tensor(wf[:, :, 2 * HEADS:3 * HEADS], wf_raw[:, :, :],
                                        wf[:, :, 0:HEADS].bitcast(f32), ALU.subtract).then_inc(s_wf, 1)
                for j in range(2):
                    dve.wait_ge(s_whi, j + 1)
                    nc.vector.tensor_tensor(w_lo[:, j, :, :], raw[:, j, :].rearrange("p (k c) -> p k c", c=P),
                                            w_hi[:, j, :, :].bitcast(f32), ALU.subtract).then_inc(s_wlo, 1)
                dve.wait_ge(s_fact, 1)
                nc.vector.scalar_tensor_tensor(f_a, ps_a[0:HEADS, :], bf[:, 0:1], f_lo, ALU.add, ALU.add).then_inc(s_f, 1)
                dve.wait_ge(s_f, 1)
                dve.wait_ge(s_fact, 2)
                seq(nc.vector.tensor_scalar(f_a, f_a, 0.0, None, ALU.min))
                dve.wait_ge(s_fact, 4)
                seq(nc.vector.tensor_tensor(f_a, f_a, f_l, ALU.subtract))
                seq(nc.vector.tensor_tensor_scan(f_c, ones_f, f_a, 0.0, ALU.mult, ALU.add))
                nc.vector.tensor_scalar(f_c, f_c, -1.0 / SCALE, None, ALU.mult).then_inc(s_c, 1)

                with dve.Fori(0, CT) as i:

                    def split_lo(r):
                        dve.wait_ge(s_whi, i * JOBS + (r + 1))
                        nc.vector.tensor_tensor(w_lo[:, r % 2, :, :], raw[:, r % 2, :].rearrange("p (k c) -> p k c", c=P),
                                                w_hi[:, r % 2, :, :].bitcast(f32), ALU.subtract).then_inc(s_wlo, 1)

                    def lo_rows(dst, src, hi, row, h):
                        rows = slice(h * HD, (h + 1) * HD)
                        to = slice((1 - h) * HD, (2 - h) * HD) if dst is q_st else rows
                        return nc.vector.scalar_tensor_tensor(dst[to, h, :], src[rows, :], prm_b[rows, row, bass.ds(i, 1)],
                                                              hi[rows, h, :].bitcast(f32), ALU.add, ALU.subtract)

                    tap = lambda j: prm_c[:, C_TAP + j, bass.ds(i, 1)]

                    def conv(j):
                        if j == 0:
                            dve.wait_ge(s_xr, i + 1)
                            nc.vector.tensor_scalar(xc[:, :], xpad[:, 0:SEQ], tap(0), prm_c[:, C_CB, bass.ds(i, 1)],
                                                    ALU.mult, ALU.add).then_inc(s_conv, 1)
                        else:
                            dve.wait_ge(s_conv, i * 4 + j)
                            nc.vector.scalar_tensor_tensor(xc[:, :], xpad[:, j:j + SEQ], tap(j), xc[:, :],
                                                           ALU.mult, ALU.add).then_inc(s_conv, 1)

                    dve.wait_ge(s_qhi, i * 2 + 1)
                    lo_rows(q_st, ps_a, q_st, B_Q, 0).then_inc(s_qlo, 1)
                    dve.wait_ge(s_qhi, i * 2 + 2)
                    lo_rows(q_st, ps_a, q_st, B_Q, 1).then_inc(s_qlo, 1)
                    split_lo(2)
                    dve.wait_ge(s_khi, i * 2 + 1)
                    lo_rows(k_lo, ps_b, k_hi, B_K, 0).then_inc(s_klo, 1)
                    dve.wait_ge(s_khi, i * 2 + 2)
                    lo_rows(k_lo, ps_b, k_hi, B_K, 1).then_inc(s_klo, 1)
                    split_lo(3)
                    split_lo(4)
                    dve.wait_ge(s_vhi, i + 1)
                    nc.vector.tensor_tensor(v_st[:, :, :, HD:P], ps_a[:, :].rearrange("p (k h c) -> p k h c", h=2, c=HD),
                                            v_st[:, :, :, 0:HD].bitcast(f32), ALU.subtract).then_inc(s_vlo, 1)

                    for s in range(STEPS + 1):
                        if 2 <= s < UNITS + 2:
                            u = s - 2
                            qb = u % QB
                            for c in range(1 + (qb >= 4)):
                                b0, b1 = 4 * c, min(4 * c + 4, qb + 1)
                                cols = slice((qb % 2) * P, (qb % 2 + 1) * P)
                                dve.wait_ge(s_phi, i * CHUNKS + (chunks_before(u) + c + 1))
                                nc.vector.tensor_tensor(pt_lo[:, b0:b1, cols],
                                                        ps_t[:, 0:(b1 - b0) * P].rearrange("p (b c) -> p b c", c=P),
                                                        pt_hi[:, b0:b1, cols].bitcast(f32), ALU.subtract).then_inc(s_plo, 1)
                        if s < UNITS:
                            n = (s % QB + 1) * P
                            if s == 0:
                                dve.wait_ge(s_cb, i * 32 + 32)
                            dve.wait_ge(s_s, i * UNITS + (s + 1))
                            dve.sem_inc(s_carry_v, 1)
                            nc.vector.tensor_tensor_reduce(probs[:, s % 3, 0:n], ps_s[:, 0:n], cb[:, s // QB, 0:n],
                                                           1.0, -3.0e38, ALU.add, ALU.max, mx[:, s:s + 1]).then_inc(s_max, 1)
                            dve.wait_ge(s_max, i * UNITS + (s + 2))
                            nc.vector.tensor_scalar(ngm[:, s:s + 1], mx[:, s:s + 1], -SCALE, None, ALU.mult).then_inc(s_neg, 1)
                        if 1 <= s < UNITS + 1:
                            u = s - 1
                            n = (u % QB + 1) * P
                            dve.wait_ge(s_exp, i * UNITS + (u + 1))
                            nc.vector.reciprocal(rinv[:, u:u + 1], rs[:, u:u + 1]).then_inc(s_rinv, 1)
                            dve.wait_ge(s_rinv, i * UNITS + (u + 1))
                            nc.vector.tensor_scalar(probs[:, u % 3, 0:n], probs[:, u % 3, 0:n], rinv[:, u:u + 1], None,
                                                    ALU.mult).then_inc(s_norm, 1)
                        if s == 0:
                            split_lo(5)
                            conv(0)
                        if s in (1, 2, 3):
                            conv(s)
                        if s == READ["GA"] + 1:
                            split_lo(6)
                        if s == READ["GR"] + 2:
                            split_lo(7)
                        if s == READ["I"] + 1:
                            dve.wait_ge(s_sq, i + 1)
                            dve.wait_ge(s_a, i + 1)
                            nc.vector.scalar_tensor_tensor(s_tl[:, :], a_t[:, :], 1.0, s_tl[:, :], ALU.add, ALU.mult).then_inc(s_rg, 1)
                        if s == READ["I"] + 2:
                            dve.wait_ge(s_rg, i * 3 + 1)
                            dve.wait_ge(s_ix, i + 1)
                            nc.vector.tensor_tensor(s_tl[:, :], s_tl[:, :], i_t[:, :], ALU.mult).then_inc(s_rg, 1)
                        if s == READ["I"] + 3:
                            dve.wait_ge(s_rg, i * 3 + 2)
                            nc.vector.tensor_tensor_scan(r_t[:, :], a_t[:, :], s_tl[:, :], 0.0, ALU.mult, ALU.add).then_inc(s_rg, 1)
                        if s == READ["I"] + 5:
                            dve.wait_ge(s_uhi, i * 2 + 1)
                            nc.vector.tensor_tensor(u_lo[:, :], r_t[:, :], u_hi[:, :].bitcast(f32), ALU.subtract).then_inc(s_ulo, 1)
                        if s == READ["MA"] + 1:
                            split_lo(8)
                        if s == READ["MR"]:
                            split_lo(9)
                        if 3 <= s < STEPS and s % 2:
                            g = (s - 3) // 2
                            rows = slice(0, HD) if g < QB // 2 else slice(HD, P)
                            q0 = (g % (QB // 2)) * 2 * P
                            dve.wait_ge(s_pvc, i * QB + (g + 1))
                            nc.vector.tensor_tensor(y_t[rows, q0:q0 + 2 * P], ps_o[rows, 0:2 * P], half[rows, :],
                                                    ALU.add).then_inc(s_pva, 1)
                    dve.wait_ge(s_uhi, i * 2 + 2)
                    nc.vector.tensor_tensor(u_lo[:, :], y_t[:, :], u_hi[:, :].bitcast(f32), ALU.subtract).then_inc(s_ulo, 1)

            @block.tensor
            def _(pe):
                pe.wait_ge(s_const, 8)
                pe.wait_ge(s_prm_in, 8 * 16)
                nc.tensor.transpose(ps_s[:, 0:64], prm_in_b[:, :], ident[0:64, 0:64]).then_inc(s_prm_t, 1)
                nc.tensor.transpose(ps_s[:, BANK:BANK + 72], prm_in[:, :], ident[0:72, 0:72]).then_inc(s_prm_t, 1)
                for t in range(TT):
                    pe.wait_ge(s_xn, t + 1)
                    if t >= 2:
                        pe.wait_ge(s_hw, t - 1)
                    for k in range(KT):
                        last = nc.tensor.transpose(pair[t % 2][:, k * P:(k + 1) * P], probs[:, t % 2, k * P:(k + 1) * P], ident[:, :])
                    last.then_inc(s_xt, 1)
                pe.wait_ge(s_hlo, TT)
                pe.wait_ge(s_wf, 3)
                for n in range(4 * KT):
                    kt, part = divmod(n, 4)
                    b = part % 2
                    last = nc.tensor.matmul(ps_a[0:3 * HEADS, b * BANK:(b + 1) * BANK], wf[:, kt, :],
                                            (r1_hi if part < 2 else r1_lo)[:, kt, b * BANK:(b + 1) * BANK],
                                            start=(kt == 0 and part < 2), stop=(kt == KT - 1 and part >= 2))
                last.then_inc(a_full, 1)
                pe.wait_ge(s_f, 1)

                with pe.Fori(0, CT) as i:

                    def weights(r):
                        pe.wait_ge(s_whi, i * JOBS + (r + 1))
                        pe.wait_ge(s_wlo, i * JOBS + (r + 3))

                    def filler(name, n):
                        if name == "GA":
                            if n == 0:
                                pe.wait_ge(s_xr, i + 1)
                                weights(J_GA)
                            mm = project(pe, J_GA % 2, ps_b, n, n + 1)
                            if n == MM - 1:
                                mm.then_inc(b_full, 1)
                        elif name == "R":
                            if n == 0:
                                pe.wait_ge(s_vlo, i + 1)
                                pe.wait_ge(s_conv, i * 4 + 4)
                                pe.wait_ge(s_gw, (i + 1) * 64)
                            mm = nc.tensor.matmul(ps_a[:, n * BANK:(n + 1) * BANK], gw[:, 0, :],
                                                  xc[:, n * BANK:(n + 1) * BANK], start=True, stop=True)
                            if n == 1:
                                mm.then_inc(a_full, 1)
                        elif name == "GR":
                            if n == 0:
                                pe.wait_ge(s_ga, i + 1)
                                weights(J_GR)
                            mm = project(pe, J_GR % 2, ps_b, n, n + 1)
                            if n == MM - 1:
                                mm.then_inc(b_full, 1)
                        elif name == "I":
                            if n == 0:
                                pe.wait_ge(s_ri, i * 2 + 2)
                            mm = nc.tensor.matmul(ps_a[:, n * BANK:(n + 1) * BANK], gw[:, 1, :],
                                                  xc[:, n * BANK:(n + 1) * BANK], start=True, stop=True)
                            if n == 1:
                                mm.then_inc(a_full, 1)
                        elif name == "MA":
                            if n == 0:
                                pe.wait_ge(s_gr, i + 1)
                                weights(J_MA)
                            mm = project(pe, J_MA % 2, ps_b, n, n + 1)
                            if n == MM - 1:
                                mm.then_inc(b_full, 1)
                        else:
                            if n == 0:
                                pe.wait_ge(s_ri, i * 2 + 3)
                                weights(J_MR)
                            mm = project(pe, J_MR % 2, ps_a, n, n + 1)
                            if n == MM - 1:
                                mm.then_inc(a_full, 1)

                    pe.wait_ge(s_sig, i * 2 + 1)
                    weights(J_Q)
                    project(pe, J_Q % 2, ps_a, 0, MM).then_inc(a_full, 1)
                    weights(J_K)
                    project(pe, J_K % 2, ps_b, 0, MM).then_inc(b_full, 1)
                    pe.wait_ge(s_qlo, i * 2 + 2)
                    weights(J_V)
                    project(pe, J_V % 2, ps_a, 0, MM).then_inc(a_full, 1)
                    pe.wait_ge(s_klo, i * 2 + 2)
                    weights(J_XR)
                    project(pe, J_XR % 2, ps_b, 0, MM).then_inc(b_full, 1)
                    pe.wait_ge(s_v, i + 1)
                    for b in range(QB):
                        last = nc.tensor.transpose(ps_a[:, b * P:(b + 1) * P], stage[:, b * P:(b + 1) * P], ident[:, :])
                    last.then_inc(a_full, 1)

                    for s in range(STEPS):
                        for c in range(2):
                            u = s - 2
                            if 0 <= u < UNITS and (c == 0 or u % QB >= 4):
                                qb = u % QB
                                b0, b1 = 4 * c, min(4 * c + 4, qb + 1)
                                pe.wait_ge(s_norm, i * UNITS + (u + 1))
                                pe.wait_ge(s_plo, i * CHUNKS + (chunks_before(u) + c + 1))
                                for b in range(b0, b1):
                                    last = nc.tensor.transpose(ps_t[:, (b - b0) * P:(b - b0 + 1) * P],
                                                               probs[:, u % 3, b * P:(b + 1) * P], ident[:, :])
                                last.then_inc(s_t, 1)
                            if c == 0:
                                for name, n in PLAN[2 * s]:
                                    filler(name, n)
                        if s < UNITS:
                            h, qb = divmod(s, QB)
                            if s == 0:
                                pe.wait_ge(s_kdup, (i + 1) * 64)
                            pe.wait_ge(s_max, i * UNITS + (s + 1))
                            for b in range(1 + (qb >= 4)):
                                n0, n1 = b * BANK, min((b + 1) * BANK, (qb + 1) * P)
                                diag = n1 == (qb + 1) * P
                                w = q_st[:, h, qb * P:(qb + 1) * P]
                                nc.tensor.matmul(ps_s[:, n0:n1], w, k_hi[:, h, n0:n1], start=True, stop=False)
                                last = nc.tensor.matmul(ps_s[:, n0:n1], w, k_lo[:, h, n0:n1], start=False, stop=not diag)
                                if diag:
                                    last = nc.tensor.matmul(ps_s[:, n1 - P:n1], ident_b[:, :], mask_b[:, :],
                                                            start=False, stop=True)
                            last.then_inc(s_s, 1)
                        for name, n in PLAN[2 * s + 1]:
                            filler(name, n)
                        if s >= 3 and s % 2:
                            g = (s - 3) // 2
                            h, gq = divmod(g, QB // 2)
                            pe.wait_ge(s_plo, i * CHUNKS + (chunks_before(2 * g + 2) + 1))
                            pe.wait_ge(s_pva, i * QB + (g + 1))
                            if g == 0:
                                pe.wait_ge(s_vlo, i + 1)
                            blocks = 2 * gq + 2
                            for kb in range(blocks):
                                c0 = P if kb == blocks - 1 else 0
                                for pt in (pt_hi, pt_lo):
                                    last = nc.tensor.matmul(ps_o[:, c0:2 * P], v_st[:, kb, h, :], pt[:, kb, c0:2 * P],
                                                            start=(kb == 0 and pt is pt_hi),
                                                            stop=(kb == blocks - 1 and pt is pt_lo))
                            last.then_inc(s_pv, 1)

        one.close()
        r2_hi = sb("r2_hi", [P, KT, SEQ], f32r)
        r2_lo = sb("r2_lo", [P, KT, SEQ], f32r)
        m_t = sb("m_t", [P, CT, SEQ])
        two = sb("two", [P, 2, SEQ])
        tmp = sb("tmp", [P, SEQ])
        wo_raw = sb("wo_raw", [P, D])
        so = sb("so", [P, 4, TT])
        u_in = [sem(f"u_in_{k}") for k in range(KT)]
        ur_in = sem("ur_in")
        sg_in = [sem("sig_in_even"), sem("sig_in_odd")]
        s_full, s_m, s_mr = sem("branch_full"), sem("m_ready"), sem("m_step")
        wo_in, s_wohi, s_wolo = sem("w_out_in"), sem("w_out_hi"), sem("w_out_lo")
        x_in = [sem("xres_in_even"), sem("xres_in_odd")]
        pw_in, s_mhi, s_mlo, s_o = sem("post_w_in"), sem("m_hi"), sem("m_lo"), sem("out_full")
        s_oss, s_ostd, s_orstd, s_onorm, s_oadd, s_oout, s_ostored = (sem(n) for n in (
            "out_sumsq", "out_std", "out_rstd", "out_scaled", "out_ready", "out_dma", "out_stored"))
        A0 = CT * JOBS
        R0 = A0 + CT
        A_FULLS = CT

        with nc.Block() as block:

            @block.sync
            def _(sp_):
                sp_.sem_inc(s_m, 2)
                sp_.sem_inc(s_onorm, 2)
                sp_.sem_inc(s_oadd, 2)
                sp_.sem_inc(s_ostored, 2)
                sp_.sem_inc(s_wolo, 1)
                for k in range(KT):
                    sp_.dma_start(r2_hi[:, k, :].bitcast(f32), ua_hi_d[k]).then_inc(u_in[k], 16)
                with sp_.Fori(1, CT // 2) as j:
                    d = j * 2
                    for e in range(2):
                        sp_.wait_ge(s_wlo, A0 + d + (e + 1))
                        sp_.dma_start(raw[:, e, :].rearrange("p (k c) -> p k c", c=P),
                                      w_a_v[:, :, bass.ds(d * P + e * P, P)]).then_inc(raw_in[e], 16)
                with sp_.Fori(0, CT // 2) as j:
                    d = j * 2
                    for e in range(2):
                        sp_.wait_ge(s_wlo, R0 + d + (e + 1))
                        sp_.dma_start(raw[:, e, :].rearrange("p (k c) -> p k c", c=P),
                                      w_r_v[:, :, bass.ds(d * P + e * P, P)]).then_inc(raw_in[e], 16)
                sp_.wait_ge(s_m, 2 * CT + 2)
                with sp_.Fori(0, TT // 2) as j:
                    t = j * 2
                    for e in range(2):
                        sp_.wait_ge(s_oadd, t + (e + 1))
                        sp_.dma_start(two[:, e, :], x_v[bass.ds(t + e, 1)].rearrange("o p c -> (o p) c")).then_inc(x_in[e], 16)

            @block.gpsimd
            def _(pool):
                for k in range(KT):
                    pool.dma_start(r1_hi[:, k, :].bitcast(f32), ur_hi_d[k]).then_inc(ur_in, 16)
                    pool.dma_start(r1_lo[:, k, :].bitcast(f32), ur_lo_d[k]).then_inc(ur_in, 16)
                for n, src in enumerate((sa_d, sr_d)):
                    with pool.Fori(0, CT // 2) as j:
                        d = j * 2
                        for e in range(2):
                            pool.wait_ge(s_m, n * CT + d + (e + 1))
                            pool.sem_inc(s_carry, 1)
                            pool.dma_start(two[:, e, :], src[bass.ds(d + e, 1)].rearrange("o p c -> (o p) c")).then_inc(sg_in[e], 16)
                with pool.Fori(0, TT // 2) as j:
                    t = j * 2
                    for e in range(2):
                        pool.wait_ge(s_onorm, t + (e + 3))
                        pool.wait_ge(x_in[e], t * 8 + 16)
                        nc.gpsimd.tensor_tensor(raw[:, e, :], raw[:, e, :], two[:, e, :], ALU.add).then_inc(s_oadd, 1)
                        pool.wait_ge(s_oadd, t + (e + 3))
                        pool.sem_inc(s_carry, 1)
                        pool.dma_start(out_v[bass.ds(t + e, 1)].rearrange("o p c -> (o p) c"), raw[:, e, :]).then_inc(s_oout, 16)
                        pool.wait_ge(s_oout, t * 16 + (16 * e + 16))
                        pool.sem_inc(s_ostored, 1)

            @block.scalar
            def _(act):
                for k in range(KT):
                    act.dma_start(r2_lo[:, k, :].bitcast(f32), ua_lo_d[k]).then_inc(u_in[k], 16)
                act.dma_start(wo_raw[:, :], w_out_v[0]).then_inc(wo_in, 16)

                def split_hi(count, e):
                    act.wait_ge(raw_in[e], count)
                    nc.scalar.activation(w_hi[:, e, :, :], raw[:, e, :].rearrange("p (k c) -> p k c", c=P), ACT.Copy).then_inc(s_whi, 1)

                with act.Fori(0, CT // 2) as j:
                    d = j * 2
                    for e in range(2):
                        act.wait_ge(s_full, d + (e + 1))
                        split_hi(d * 8 + (A0 * 8 + 32), e)

                def branch_r(d, e, more):
                    act.wait_ge(wo_in, (d + e) * 16 + 16)
                    nc.scalar.activation(r2_hi[:, d + e, :] if isinstance(d, int) else r2_hi[:, bass.ds(d + e, 1), :].rearrange("p o c -> p (o c)"),
                                         wo_raw[:, :], ACT.Copy).then_inc(s_wohi, 1)
                    act.wait_ge(s_full, d + (CT + e + 1))
                    if more:
                        split_hi(d * 8 + (R0 * 8 + 32), e)
                    if more or e == 0:
                        act.wait_ge(s_wolo, d + (e + 2))
                        act.dma_start(wo_raw[:, :], w_out_v[d + e + 1] if isinstance(d, int)
                                      else w_out_v[bass.ds(d + (e + 1), 1)].rearrange("o p c -> (o p) c")).then_inc(wo_in, 16)

                with act.Fori(0, (CT - 2) // 2) as j:
                    d = j * 2
                    for e in range(2):
                        branch_r(d, e, True)
                for e in range(2):
                    branch_r(CT - 2, e, False)
                act.wait_ge(s_wolo, CT + 1)
                act.dma_start(wo_raw[:, :], post_w[0:1, :].to_broadcast([P, D])).then_inc(pw_in, 16)

                def m_hi(t, e):
                    nc.scalar.activation(r1_hi[:, e, :].rearrange("p (k c) -> p k c", c=P),
                                         m_t[:, :, bass.ds(t * P + e * P, P)], ACT.Copy).then_inc(s_mhi, 1)

                def out_stats(t, e):
                    act.wait_ge(s_o, t + (e + 1))
                    nc.scalar.activation(tmp[:, :], pair[e][:, :], ACT.Square,
                                         accum_out=so[:, 0, bass.ds(t + e, 1)]).then_inc(s_oss, 1)
                    act.wait_ge(s_oss, 2 * t + (2 * e + 2))
                    nc.scalar.activation(so[:, 2, bass.ds(t + e, 1)], so[:, 1, bass.ds(t + e, 1)], ACT.Sqrt).then_inc(s_ostd, 1)

                act.wait_ge(s_m, 2 * CT + 2)
                m_hi(0, 0)
                m_hi(0, 1)
                with act.Fori(0, (TT - 2) // 2) as j:
                    t = j * 2
                    for e in range(2):
                        out_stats(t, e)
                        m_hi(t + 2, e)
                for e in range(2):
                    out_stats(TT - 2, e)

            @block.vector
            def _(dve):
                def split_lo(count, e):
                    dve.wait_ge(s_whi, count)
                    nc.vector.tensor_tensor(w_lo[:, e, :, :], raw[:, e, :].rearrange("p (k c) -> p k c", c=P),
                                            w_hi[:, e, :, :].bitcast(f32), ALU.subtract).then_inc(s_wlo, 1)

                with dve.Fori(0, CT // 2) as j:
                    d = j * 2
                    for e in range(2):
                        dve.wait_ge(s_full, d + (e + 1))
                        dve.wait_ge(sg_in[e], d * 8 + 16)
                        nc.vector.tensor_tensor(m_t[:, bass.ds(d + e, 1), :].rearrange("p o c -> p (o c)"), pair[e][:, :],
                                                two[:, e, :], ALU.mult).then_inc(s_m, 1)
                        split_lo(d + (A0 + e + 3), e)

                def branch_r(d, e, more):
                    dve.wait_ge(s_wohi, d + (e + 1))
                    row = lambda z: z[:, bass.ds(d + e, 1), :].rearrange("p o c -> p (o c)")
                    nc.vector.tensor_tensor(row(r2_lo), wo_raw[:, :], row(r2_hi).bitcast(f32), ALU.subtract).then_inc(s_wolo, 1)
                    dve.wait_ge(s_full, d + (CT + e + 1))
                    dve.wait_ge(sg_in[e], d * 8 + (CT * 8 + 16))
                    dve.wait_ge(s_m, d + (CT + e + 2))
                    nc.vector.tensor_tensor(tmp[:, :], pair[e][:, :], two[:, e, :], ALU.mult).then_inc(s_mr, 1)
                    dve.wait_ge(s_mr, d + (e + 1))
                    nc.vector.tensor_tensor(row(m_t), row(m_t), tmp[:, :], ALU.add).then_inc(s_m, 1)
                    if more:
                        split_lo(d + (R0 + e + 3), e)

                with dve.Fori(0, (CT - 2) // 2) as j:
                    d = j * 2
                    for e in range(2):
                        branch_r(d, e, True)
                for e in range(2):
                    branch_r(CT - 2, e, False)

                def m_lo(t, e):
                    dve.wait_ge(s_mhi, t + (e + 1))
                    nc.vector.tensor_tensor(r1_lo[:, e, :].rearrange("p (k c) -> p k c", c=P),
                                            m_t[:, :, bass.ds(t * P + e * P, P)],
                                            r1_hi[:, e, :].rearrange("p (k c) -> p k c", c=P).bitcast(f32),
                                            ALU.subtract).then_inc(s_mlo, 1)

                def finish(t, e):
                    c = lambda k: so[:, k, bass.ds(t + e, 1)]
                    dve.wait_ge(s_oss, 2 * t + (2 * e + 1))
                    nc.vector.tensor_scalar(c(1), c(0), 1.0 / D, EPS, ALU.mult, ALU.add).then_inc(s_oss, 1)
                    dve.wait_ge(s_ostd, t + (e + 1))
                    nc.vector.reciprocal(c(3), c(2)).then_inc(s_orstd, 1)
                    dve.wait_ge(s_orstd, t + (e + 1))
                    dve.wait_ge(s_ostored, t + (e + 1))
                    nc.vector.scalar_tensor_tensor(raw[:, e, :], pair[e][:, :], c(3), wo_raw[:, :],
                                                   ALU.mult, ALU.mult).then_inc(s_onorm, 1)

                dve.wait_ge(s_m, 2 * CT + 2)
                m_lo(0, 0)
                m_lo(0, 1)
                dve.wait_ge(pw_in, 16)
                with dve.Fori(0, (TT - 2) // 2) as j:
                    t = j * 2
                    for e in range(2):
                        finish(t, e)
                        m_lo(t + 2, e)
                for e in range(2):
                    finish(TT - 2, e)

            @block.tensor
            def _(pe):
                def branch(d, e, n, hi, lo):
                    pe.wait_ge(s_whi, d + ((A0, R0)[n] + e + 1))
                    pe.wait_ge(s_wlo, d + ((A0, R0)[n] + e + 3))
                    pe.wait_ge(s_m, d + (n * CT + e + 1))
                    for kt in range(KT):
                        if n == 0:
                            pe.wait_ge(u_in[kt], 32)
                        for part in range(6):
                            w = (w_hi if part < 4 else w_lo)[:, e, kt, :]
                            u = lo if part in (2, 3) else hi
                            cols = slice((part % 2) * BANK, (part % 2 + 1) * BANK)
                            last = nc.tensor.matmul(pair[e][:, cols], w, u[:, kt, cols],
                                                    start=(kt == 0 and part < 2), stop=(kt == KT - 1 and part >= 4))
                    last.then_inc(s_full, 1)

                with pe.Fori(0, CT // 2) as j:
                    d = j * 2
                    for e in range(2):
                        branch(d, e, 0, r2_hi, r2_lo)
                pe.wait_ge(ur_in, 2 * KT * 16)
                with pe.Fori(0, CT // 2) as j:
                    d = j * 2
                    for e in range(2):
                        branch(d, e, 1, r1_hi, r1_lo)
                pe.wait_ge(s_wolo, CT + 1)
                with pe.Fori(0, TT // 2) as j:
                    t = j * 2
                    for e in range(2):
                        pe.wait_ge(s_mlo, t + (e + 1))
                        pe.wait_ge(s_onorm, t + (e + 1))
                        for kt in range(KT):
                            for part in range(6):
                                m = (r1_hi if part < 4 else r1_lo)[:, e, kt * P:(kt + 1) * P]
                                w = r2_lo if part in (2, 3) else r2_hi
                                cols = slice((part % 2) * BANK, (part % 2 + 1) * BANK)
                                last = nc.tensor.matmul(pair[e][:, cols], m, w[:, kt, cols],
                                                        start=(kt == 0 and part < 2), stop=(kt == KT - 1 and part >= 4))
                        last.then_inc(s_o, 1)


_INS = ["x", "pre_norm_w", "w_in", "b_in", "conv_w", "conv_b", "rg_wa", "rg_ba", "rg_wx", "rg_bx",
        "rg_lambda", "w_branch_a", "w_branch_r", "w_out", "post_norm_w"]


def kernel(**inputs):
    import numpy as _np
    import concourse.bacc as _bacc
    from concourse import mybir as _mybir
    from concourse.bass_utils import run_bass_kernel_spmd as _run

    nc = _bacc.Bacc("TRN2", target_bir_lowering=False, num_devices=1)
    arrays, args = {}, []
    for name in _INS:
        a = _np.ascontiguousarray(inputs[name])
        arrays[f"in_{name}"] = a
        args.append(nc.dram_tensor(f"in_{name}", a.shape, _mybir.dt.from_np(a.dtype), kind="ExternalInput").ap())
    args.append(nc.dram_tensor("out_0", (1, SEQ, D), _mybir.dt.float32, kind="ExternalOutput").ap())
    build(nc, *args)
    r = _run(nc, [arrays], core_ids=[0])
    return r.results[0]["out_0"]
```

```python
import concourse.bass as bass
from concourse import mybir
from contextlib import ExitStack

P = 128
D = 1024
SEQ = 1024
KT = D // P
TT = SEQ // P
CT = D // P
HD = 64
HEADS = D // HD
QB = SEQ // P
UNITS = 2 * QB
BANK = 512
EPS = 1e-6
RG_C = 8.0
MASK = -1e30
SCALE = HD ** -0.5

Q_COL, K_COL, V_COL, F_COL = 0, D, 2 * D, 3 * D
GA_COL = 3 * D + HEADS
XR_COL, GR_COL, MA_COL, MR_COL = (GA_COL + n * D for n in (1, 2, 3, 4))
JOB_COLS = [XR_COL, K_COL, Q_COL, V_COL, GA_COL, GR_COL, MA_COL, MR_COL]
J_XR, J_K, J_Q, J_V, J_GA, J_GR, J_MA, J_MR = range(8)
JOBS = 8
B_Q, B_K, B_V, B_GA, B_XR, B_GR, B_MA, B_MR = range(8)
C_TAP, C_CB, C_BA, C_BX, C_LAM, C_PRE = 0, 4, 5, 6, 7, 8

MM = 6 * KT
A_K, A_V, A_VT, A_GR, A_MR, FILLS_A = 1, 2, 3, 4, 5, 5
B_XR_, B_Q_, B_GA_, B_MA_, FILLS_B = 1, 2, 3, 4, 4
CHUNKS = 2 * sum(1 + (b >= 4) for b in range(QB))
LAG = 3
STEPS = UNITS + LAG


def chunks_before(u):
    return sum(1 + (v % QB >= 4) for v in range(u))


def filler_plan():
    seq = [(name, n) for name in ("GA", "GR", "MA", "MR") for n in range(MM)]
    share = []
    for s in range(STEPS):
        two = s >= LAG and (s - LAG) % QB >= 4
        share += [8 if two and s >= UNITS else 5 if two else 4, 7 if two and s % 2 == 0 else 5]
    total = sum(share)
    plan, read, at = [], {}, 0
    for s in range(2 * STEPS):
        part = []
        while at < len(seq) and at * total < len(seq) * sum(share[:s + 1]):
            part.append(seq[at])
            read[seq[at][0]] = (s + 1) // 2
            at += 1
        plan.append(part)
    return plan, read


PLAN, READ = filler_plan()


def build(nc, x, pre_w, w_in, b_in, conv_w, conv_b, rg_wa, rg_ba, rg_wx, rg_bx, lam, w_a, w_r,
          w_out, post_w, out):
    f32, f32r, bf16 = mybir.dt.float32, mybir.dt.float32r, mybir.dt.bfloat16
    ACT, ALU = mybir.ActivationFunctionType, mybir.AluOpType

    w_in_v = w_in[0].rearrange("(k p) c -> p k c", p=P)
    w_a_v = w_a[0].rearrange("(k p) c -> p k c", p=P)
    w_r_v = w_r[0].rearrange("(k p) c -> p k c", p=P)
    w_out_v = w_out[0].rearrange("(k p) c -> k p c", p=P)
    x_v = x[0].rearrange("(t p) d -> t p d", p=P)
    out_v = out[0].rearrange("(t p) d -> t p d", p=P)

    ua_d, ur_d = (nc.dram_tensor(f"{n}_scratch", (CT, P, SEQ), f32, kind="Internal").ap() for n in ("u_a", "u_r"))
    sig_d = nc.dram_tensor("merge_gate_scratch", (2 * CT, P, SEQ), f32, kind="Internal").ap()
    c_d = nc.dram_tensor("c_scratch", (HEADS, SEQ), f32, kind="Internal").ap()

    ctx = ExitStack()
    with ctx:
        def sb(name, shape, dt=f32, stack=ctx):
            return stack.enter_context(nc.sbuf_tensor(name, shape, dt))

        def sem(name):
            return ctx.enter_context(nc.semaphore(name))

        r1_hi = sb("r1_hi", [P, KT, SEQ], f32r)
        r1_lo = sb("r1_lo", [P, KT, SEQ], f32r)
        raw = sb("raw", [P, 2, KT * P])
        w_hi = sb("w_hi", [P, 2, KT, P], f32r)
        w_lo = sb("w_lo", [P, 2, KT, P], f32r)
        ident = sb("ident", [P, P])
        ident_b = sb("ident_b", [P, P], bf16)
        mask_b = sb("mask_b", [P, P], bf16)
        prm_b = sb("prm_b", [P, 8, CT])
        prm_c = sb("prm_c", [P, 9, CT])
        rgk = sb("rgk", [P, 2, CT])

        ps_a = ctx.enter_context(nc.psum_tensor("ps_a", [P, 2 * BANK], f32))
        ps_b = ctx.enter_context(nc.psum_tensor("ps_b", [P, 2 * BANK], f32))
        ps_s = ctx.enter_context(nc.psum_tensor("ps_s", [P, 2 * BANK], f32))
        ps_t = ctx.enter_context(nc.psum_tensor("ps_t", [P, BANK], f32))
        ps_o = ctx.enter_context(nc.psum_tensor("ps_o", [P, BANK], f32))
        pair = [ps_a, ps_b]

        raw_in = [sem("raw_in_even"), sem("raw_in_odd")]
        s_whi, s_wlo = sem("w_hi_ready"), sem("w_lo_ready")
        s_carry, s_carry_v, s_carry_s = (sem(f"wait_carrier_{e}") for e in ("pool", "vector", "sync"))
        s_const, s_prm_in, s_prm_t, s_prm = sem("consts"), sem("params_in"), sem("params_t"), sem("params")
        s_x = [sem(f"x_in_{t}") for t in range(TT)]
        s_ss, s_var, s_std, s_rstd, s_xn = sem("sumsq"), sem("mean_square"), sem("std"), sem("rstd"), sem("x_scaled")
        s_xt, s_hw, s_hhi, s_hlo = sem("x_transposed"), sem("h_weighted"), sem("h_hi"), sem("h_lo")
        s_pro = sem("dve_prologue_step")
        s_wf_in, s_wf, s_f, s_fact, s_c, s_c_out = (sem(n) for n in (
            "wf_in", "wf_split", "f_summed", "f_act", "c_ready", "c_stored"))
        s_sp = sem("softplus_act")
        a_full, b_full = sem("pair_a_full"), sem("pair_b_full")
        s_qhi, s_qlo, s_khi, s_klo, s_kdup, s_v, s_vhi, s_vlo = (sem(n) for n in (
            "q_hi", "q_lo", "k_hi", "k_lo", "k_dup", "v_sb", "v_hi", "v_lo"))
        s_s, s_max, s_neg, s_exp = sem("scores_ready"), sem("row_max"), sem("neg_max"), sem("exp_done")
        s_rinv, s_norm = sem("row_sum_inv"), sem("probs_ready")
        s_t, s_phi, s_plo = sem("probs_t"), sem("p_hi"), sem("p_lo")
        s_pv, s_pvc, s_pva = sem("values_ready"), sem("values_half"), sem("values_added")
        s_cb = sem("c_broadcast_in")
        s_xr, s_conv, s_gw = sem("xr_padded"), sem("conv_step"), sem("gate_weights_in")
        s_ri, s_tanh, s_sq, s_a = sem("r_i_ready"), sem("tanh_ready"), sem("sqrt_ready"), sem("decay_ready")
        s_gp = sem("gate_products")
        s_ix, s_rg = sem("i_times_x"), sem("rg_step")
        s_gaz, s_grz, s_maz = sem("gate_a_linear"), sem("gate_r_linear"), sem("merge_a_linear")
        s_ga, s_gr, s_sig, s_sigr = sem("gate_a_ready"), sem("gate_r_ready"), sem("merge_a_ready"), sem("merge_r_ready")
        s_ur, s_ua, s_uout, s_sigout = sem("ur_ready"), sem("ua_ready"), sem("u_stored"), sem("merge_gate_stored")
        s_stored = sem("iteration_stored")

        one = ExitStack()
        pt_hi = sb("pt_hi", [P, QB, 2 * P], f32r, one)
        pt_lo = sb("pt_lo", [P, QB, 2 * P], f32r, one)
        q_st = sb("q_st", [P, 2, SEQ], f32r, one)
        k_hi = sb("k_hi", [P, 2, SEQ], f32r, one)
        k_lo = sb("k_lo", [P, 2, SEQ], f32r, one)
        v_st = sb("v_st", [P, QB, 2, P], f32r, one)
        probs = sb("probs", [P, 3, SEQ], f32, one)
        cb = sb("cb", [P, 2, SEQ], f32, one)
        stage = sb("stage", [P, SEQ], f32, one)
        gate_a = sb("gate_a", [P, SEQ], f32, one)
        y_t = sb("y_t", [P, SEQ], f32, one)
        half = sb("half", [P, 2 * P], f32, one)
        gate_m = sb("gate_m", [P, SEQ], f32, one)
        PAD = 3
        xpad = sb("xpad", [P, PAD + SEQ], f32, one)
        xc = sb("xc", [P, SEQ], f32, one)
        r_t = sb("r_t", [P, SEQ], f32, one)
        i_t = sb("i_t", [P, SEQ], f32, one)
        a_t = sb("a_t", [P, SEQ], f32, one)
        s_tl = sb("s_tl", [P, SEQ], f32, one)
        gw = sb("gw", [P, 2, P], f32, one)
        mx = sb("mx", [P, UNITS], f32, one)
        ngm = sb("ngm", [P, UNITS], f32, one)
        rs = sb("rs", [P, UNITS], f32, one)
        rinv = sb("rinv", [P, UNITS], f32, one)
        st8 = sb("st8", [P, 4, TT], f32, one)
        wf_raw = sb("wf_raw", [P, KT, HEADS], f32, one)
        wf = sb("wf", [P, KT, 3 * HEADS], f32r, one)
        bf = sb("bf", [HEADS, 1], f32, one)
        sp = sb("sp", [P, 5, CT], f32, one)
        prm_in = sb("prm_in", [72, P], f32, one)
        prm_in_b = sb("prm_in_b", [64, P], f32, one)
        x_sb = [probs[:, 0, :], probs[:, 1, :], probs[:, 2, :], i_t[:, :], a_t[:, :], s_tl[:, :], gate_a[:, :], y_t[:, :]]
        h_sb = [stage, xc]
        f_lo, f_a, f_b, f_l, f_c = (z[0:HEADS, :] for z in (xc, i_t, a_t, s_tl, r_t))
        ones_f = y_t[0:HEADS, :]

        def project(pe, slot, dst, first, last):
            for n in range(first, last):
                kt, part = divmod(n, 6)
                w = (w_hi if part < 4 else w_lo)[:, slot, kt, :]
                h = r1_lo if part in (2, 3) else r1_hi
                b = part % 2
                mm = nc.tensor.matmul(dst[:, b * BANK:(b + 1) * BANK], w,
                                      h[:, kt, b * BANK:(b + 1) * BANK],
                                      start=(kt == 0 and part < 2), stop=(kt == KT - 1 and part >= 4))
            return mm

        with nc.Block() as block:

            @block.sync
            def _(sp_):
                for s in (s_max, s_stored, s_maz, s_ur, s_ri, s_pva, s_plo):
                    sp_.sem_inc(s, 1)
                sp_.sem_inc(s_wlo, 2)
                sp_.dma_start(prm_in_b[0:24, :], b_in[0, 0:3 * D].rearrange("(r c) -> r c", c=P)).then_inc(s_prm_in, 16)
                sp_.dma_start(prm_in_b[24:64, :], b_in[0, GA_COL:GA_COL + 5 * D].rearrange("(r c) -> r c", c=P)).then_inc(s_prm_in, 16)
                sp_.dma_start(prm_in[0:32, :], conv_w[0].rearrange("j (r c) -> (j r) c", c=P)).then_inc(s_prm_in, 16)
                for n, v in enumerate((conv_b, rg_ba, rg_bx, lam, pre_w)):
                    sp_.dma_start(prm_in[32 + 8 * n:40 + 8 * n, :], v[0].rearrange("(r c) -> r c", c=P)).then_inc(s_prm_in, 16)
                for t in range(0, TT, 2):
                    sp_.dma_start(x_sb[t], x_v[t]).then_inc(s_x[t], 16)
                sp_.dma_start(wf_raw[:, :, :], w_in_v[:, :, F_COL:F_COL + HEADS]).then_inc(s_wf_in, 16)
                sp_.dma_start(bf[:, :], b_in[0, F_COL:F_COL + HEADS].rearrange("(h o) -> h o", o=1)).then_inc(s_wf_in, 16)
                with sp_.Fori(0, CT) as i:
                    for r in range(JOBS):
                        src = w_in_v[:, :, bass.ds(i * P + JOB_COLS[r], P)]
                        sp_.wait_ge(s_wlo, i * JOBS + (r + 1))
                        sp_.sem_inc(s_carry_s, 1)
                        sp_.dma_start(raw[:, r % 2, :].rearrange("p (k c) -> p k c", c=P), src).then_inc(raw_in[r % 2], 16)

                for r in range(2):
                    sp_.wait_ge(s_wlo, CT * JOBS + (r + 1))
                    sp_.dma_start(raw[:, r, :].rearrange("p (k c) -> p k c", c=P),
                                  w_a_v[:, :, r * P:(r + 1) * P]).then_inc(raw_in[r], 16)

            @block.gpsimd
            def _(pool):
                nc.gpsimd.memset(ident[:, :], 0.0).then_inc(s_const, 1)
                nc.gpsimd.memset(ident_b[:, :], 0.0).then_inc(s_const, 1)
                nc.gpsimd.memset(mask_b[:, :], 0.0).then_inc(s_const, 1)
                pool.wait_ge(s_const, 3)
                for m in (ident, ident_b):
                    nc.gpsimd.affine_select(out=m[:, :], in_=m[:, :], compare_op=ALU.not_equal, fill=1.0,
                                            base=0, pattern=[[-1, P]], channel_multiplier=1).then_inc(s_const, 1)
                nc.gpsimd.affine_select(out=mask_b[:, :], in_=mask_b[:, :], compare_op=ALU.is_ge, fill=MASK,
                                        base=0, pattern=[[-1, P]], channel_multiplier=1).then_inc(s_const, 1)
                nc.gpsimd.memset(gw[:, :, :], 0.0).then_inc(s_const, 1)
                nc.gpsimd.memset(xpad[:, 0:PAD], 0.0).then_inc(s_const, 1)
                pool.wait_ge(s_const, 8)
                pool.wait_ge(s_c, 1)
                pool.dma_start(c_d, f_c).then_inc(s_c_out, 16)
                pool.wait_ge(s_c_out, 16)
                with pool.Fori(0, CT) as i:
                    pool.wait_ge(s_max, i * UNITS + 1)
                    pool.sem_inc(s_carry, 1)
                    for h in range(2):
                        pool.dma_start(cb[:, h, :], c_d[bass.ds(i * 2 + h, 1), :].to_broadcast([P, SEQ])).then_inc(s_cb, 16)
                    pool.wait_ge(s_ri, i * 3 + 1)
                    pool.sem_inc(s_carry, 1)
                    for g, w in enumerate((rg_wa, rg_wx)):
                        for b in range(2):
                            pool.dma_start(gw[b * HD:(b + 1) * HD, g, b * HD:(b + 1) * HD],
                                           w[0, bass.ds(i * 2 + b, 1), :, :].rearrange("o a b -> (o a) b")).then_inc(s_gw, 16)
                    pool.wait_ge(s_klo, i * 2 + 2)
                    pool.sem_inc(s_carry, 1)
                    for t in (k_hi, k_lo):
                        pool.dma_start(t[HD:P, 0, :].bitcast(f32), t[0:HD, 0, :].bitcast(f32)).then_inc(s_kdup, 16)
                        pool.dma_start(t[0:HD, 1, :].bitcast(f32), t[HD:P, 1, :].bitcast(f32)).then_inc(s_kdup, 16)
                    pool.wait_ge(s_ri, i * 3 + 4)
                    pool.wait_ge(s_conv, i * 4 + 4)
                    nc.gpsimd.tensor_tensor(i_t[:, :], i_t[:, :], xc[:, :], ALU.mult).then_inc(s_ix, 1)
                    pool.wait_ge(s_gr, i + 1)
                    pool.wait_ge(s_rg, i * 3 + 3)
                    nc.gpsimd.tensor_tensor(r_t[:, :], r_t[:, :], xpad[:, PAD:], ALU.mult).then_inc(s_ur, 1)
                    pool.wait_ge(s_ur, i + 2)
                    pool.sem_inc(s_carry, 1)
                    pool.dma_start(ur_d[bass.ds(i, 1)].rearrange("o p c -> (o p) c"), r_t[:, :]).then_inc(s_uout, 16)
                    pool.wait_ge(s_pva, i * QB + (QB + 1))
                    pool.wait_ge(s_ga, i + 1)
                    nc.gpsimd.tensor_tensor(y_t[:, :], y_t[:, :], gate_a[:, :], ALU.mult).then_inc(s_ua, 1)
                    pool.wait_ge(s_ua, i + 1)
                    pool.sem_inc(s_carry, 1)
                    pool.dma_start(ua_d[bass.ds(i, 1)].rearrange("o p c -> (o p) c"), y_t[:, :]).then_inc(s_uout, 16)
                    pool.wait_ge(s_sig, i + 1)
                    pool.sem_inc(s_carry, 1)
                    pool.dma_start(sig_d[bass.ds(i, 1)].rearrange("o p c -> (o p) c"), stage[:, :]).then_inc(s_sigout, 16)
                    pool.wait_ge(s_sigr, i + 2)
                    pool.sem_inc(s_carry, 1)
                    pool.dma_start(sig_d[bass.ds(i + CT, 1)].rearrange("o p c -> (o p) c"), gate_m[:, :]).then_inc(s_sigout, 16)
                    pool.wait_ge(s_uout, i * 32 + 32)
                    pool.wait_ge(s_sigout, i * 32 + 32)
                    pool.sem_inc(s_stored, 1)

            @block.scalar
            def _(act):
                for t in range(1, TT, 2):
                    act.dma_start(x_sb[t], x_v[t]).then_inc(s_x[t], 16)
                for s in range(TT + 2):
                    if s < TT:
                        act.wait_ge(s_x[s], 16)
                        if s:
                            act.wait_ge(s_ss, s)
                        nc.scalar.activation(r_t[:, :], x_sb[s], ACT.Square, accum_out=st8[:, 0, s:s + 1]).then_inc(s_ss, 1)
                    if 1 <= s <= TT:
                        t = s - 1
                        act.wait_ge(s_var, t + 1)
                        nc.scalar.activation(st8[:, 2, t:t + 1], st8[:, 1, t:t + 1], ACT.Sqrt).then_inc(s_std, 1)
                        act.wait_ge(s_rstd, t + 1)
                        nc.scalar.activation(x_sb[t], x_sb[t], ACT.Identity, scale=st8[:, 3, t:t + 1]).then_inc(s_xn, 1)
                    if s >= 2:
                        t = s - 2
                        act.wait_ge(s_hw, t + 1)
                        nc.scalar.activation(r1_hi[:, :, t * P:(t + 1) * P],
                                             h_sb[t % 2][:, :].rearrange("p (k c) -> p k c", c=P), ACT.Copy).then_inc(s_hhi, 1)
                act.wait_ge(s_wf_in, 32)
                act.wait_ge(s_wf, 1)
                nc.scalar.activation(wf[:, :, 0:HEADS], wf_raw[:, :, :], ACT.Copy).then_inc(s_wf, 1)
                for j in range(2):
                    act.wait_ge(raw_in[j], 16)
                    nc.scalar.activation(w_hi[:, j, :, :], raw[:, j, :].rearrange("p (k c) -> p k c", c=P), ACT.Copy).then_inc(s_whi, 1)
                act.wait_ge(s_pro, 3)
                nc.scalar.activation(sp[:, 0, :], sp[:, 1, :], ACT.Exp, scale=-1.0).then_inc(s_sp, 1)
                act.wait_ge(a_full, 1)
                nc.scalar.activation(f_lo, ps_a[2 * HEADS:3 * HEADS, :], ACT.Identity).then_inc(s_fact, 1)
                act.wait_ge(s_f, 1)
                nc.scalar.activation(f_b, f_a, ACT.Abs).then_inc(s_fact, 1)
                act.wait_ge(s_fact, 2)
                nc.scalar.activation(f_b, f_b, ACT.Exp, scale=-1.0).then_inc(s_fact, 1)
                act.wait_ge(s_fact, 3)
                nc.scalar.activation(f_l, f_b, ACT.Ln, bias=1.0).then_inc(s_fact, 1)

                with act.Fori(0, CT) as i:

                    def split_hi(r):
                        act.wait_ge(raw_in[r % 2], i * (JOBS * 8) + 16 * (r // 2 + 1))
                        nc.scalar.activation(w_hi[:, r % 2, :, :], raw[:, r % 2, :].rearrange("p (k c) -> p k c", c=P),
                                             ACT.Copy).then_inc(s_whi, 1)

                    bias = lambda row: prm_b[:, row, bass.ds(i, 1)]
                    bias_c = lambda row: prm_c[:, row, bass.ds(i, 1)]
                    act.wait_ge(b_full, i * FILLS_B + B_XR_)
                    act.wait_ge(s_ur, i + 1)
                    nc.scalar.activation(xpad[:, PAD:], ps_b[:, :], ACT.Identity, bias=bias(B_XR)).then_inc(s_xr, 1)
                    split_hi(2)
                    act.wait_ge(a_full, i * FILLS_A + (A_K + 1))
                    for h in range(2):
                        rows = slice(h * HD, (h + 1) * HD)
                        nc.scalar.activation(k_hi[rows, h, :], ps_a[rows, :], ACT.Identity,
                                             bias=prm_b[rows, B_K, bass.ds(i, 1)]).then_inc(s_khi, 1)
                    split_hi(3)
                    act.wait_ge(s_gp, i * 2 + 1)
                    act.wait_ge(s_stored, i + 1)
                    nc.scalar.activation(r_t[:, :], ps_s[:, :], ACT.Sigmoid, bias=bias_c(C_BA)).then_inc(s_ri, 1)
                    act.wait_ge(s_gp, i * 2 + 2)
                    for b, ps in enumerate((ps_t, ps_o)):
                        nc.scalar.activation(i_t[:, b * BANK:(b + 1) * BANK], ps[:, :], ACT.Sigmoid, bias=bias_c(C_BX)).then_inc(s_ri, 1)
                    act.wait_ge(s_ri, i * 3 + 2)
                    nc.scalar.activation(s_tl[:, :], r_t[:, :], ACT.Tanh, scale=rgk[:, 1, bass.ds(i, 1)]).then_inc(s_tanh, 1)
                    act.wait_ge(b_full, i * FILLS_B + B_Q_)
                    for h in range(2):
                        rows = slice(h * HD, (h + 1) * HD)
                        nc.scalar.activation(q_st[rows, h, :], ps_b[rows, :], ACT.Identity,
                                             bias=prm_b[rows, B_Q, bass.ds(i, 1)]).then_inc(s_qhi, 1)
                    split_hi(4)
                    act.wait_ge(s_tanh, i + 1)
                    nc.scalar.activation(s_tl[:, :], s_tl[:, :], ACT.Sqrt).then_inc(s_sq, 1)
                    nc.scalar.activation(a_t[:, :], r_t[:, :], ACT.Exp, scale=rgk[:, 0, bass.ds(i, 1)]).then_inc(s_a, 1)
                    act.wait_ge(a_full, i * FILLS_A + (A_V + 1))
                    nc.scalar.activation(stage[:, :], ps_a[:, :], ACT.Identity, bias=bias(B_V)).then_inc(s_v, 1)
                    split_hi(5)

                    for s in range(STEPS + 1):
                        for c in range(2):
                            u = s - LAG
                            qb = u % QB
                            if 0 <= u < UNITS and (c == 0 or qb >= 4):
                                b0, b1 = 4 * c, min(4 * c + 4, qb + 1)
                                act.wait_ge(s_t, i * CHUNKS + (chunks_before(u) + c + 1))
                                nc.scalar.activation(pt_hi[:, b0:b1, (qb % 2) * P:(qb % 2 + 1) * P],
                                                     ps_t[:, 0:(b1 - b0) * P].rearrange("p (b c) -> p b c", c=P),
                                                     ACT.Copy).then_inc(s_phi, 1)
                            u = s - 1
                            if c == 0 and 0 <= u < UNITS:
                                n = (u % QB + 1) * P
                                act.wait_ge(s_neg, i * UNITS + (u + 1))
                                nc.scalar.activation(probs[:, u % 3, 0:n], probs[:, u % 3, 0:n], ACT.Exp, scale=SCALE,
                                                     bias=ngm[:, u:u + 1], accum_out=rs[:, u:u + 1]).then_inc(s_exp, 1)
                        if s == 1:
                            act.wait_ge(a_full, i * FILLS_A + (A_VT + 1))
                            nc.scalar.activation(v_st[:, :, :, 0:HD],
                                                 ps_a[:, :].rearrange("p (k h c) -> p k h c", h=2, c=HD), ACT.Copy).then_inc(s_vhi, 1)
                        if s == READ["GA"]:
                            act.wait_ge(b_full, i * FILLS_B + B_GA_)
                            nc.scalar.activation(gate_a[:, :], ps_b[:, :], ACT.Identity, bias=bias(B_GA)).then_inc(s_gaz, 1)
                        if s == READ["GA"] + 1:
                            split_hi(6)
                        if s == READ["GR"]:
                            act.wait_ge(a_full, i * FILLS_A + (A_GR + 1))
                            act.wait_ge(s_conv, i * 4 + 4)
                            nc.scalar.activation(xpad[:, PAD:], ps_a[:, :], ACT.Identity, bias=bias(B_GR)).then_inc(s_grz, 1)
                        if s == READ["GR"] + 1:
                            split_hi(7)
                        if s == READ["MA"]:
                            act.wait_ge(b_full, i * FILLS_B + B_MA_)
                            nc.scalar.activation(stage[:, :], ps_b[:, :], ACT.Identity, bias=bias(B_MA)).then_inc(s_maz, 1)
                        if s == READ["MA"] + 1:
                            split_hi(8)
                        if 4 <= s < STEPS and s % 2 == 0:
                            g = (s - 4) // 2
                            mine, other = (slice(0, HD), slice(HD, P)) if g < QB // 2 else (slice(HD, P), slice(0, HD))
                            act.wait_ge(s_pv, i * QB + (g + 1))
                            nc.scalar.activation(half[mine, :], ps_o[other, 0:2 * P], ACT.Copy).then_inc(s_pvc, 1)
                        if s == UNITS + 1:
                            act.wait_ge(s_grz, i + 1)
                            nc.scalar.activation(xpad[:, PAD:], xpad[:, PAD:], ACT.Silu).then_inc(s_gr, 1)
                        if s == UNITS + 2:
                            act.wait_ge(s_gaz, i + 1)
                            nc.scalar.activation(gate_a[:, :], gate_a[:, :], ACT.Silu).then_inc(s_ga, 1)
                        if s == STEPS:
                            act.wait_ge(a_full, i * FILLS_A + (A_MR + 1))
                            split_hi(9)
                            nc.scalar.activation(gate_m[:, :], ps_a[:, :], ACT.Sigmoid, bias=bias(B_MR)).then_inc(s_sigr, 1)
                            act.wait_ge(s_maz, i + 2)
                            nc.scalar.activation(stage[:, :], stage[:, :], ACT.Sigmoid).then_inc(s_sig, 1)

            @block.vector
            def _(dve):
                pro = [0]

                def seq(ins):
                    pro[0] += 1
                    ins.then_inc(s_pro, 1)
                    dve.wait_ge(s_pro, pro[0])

                dve.wait_ge(s_prm_t, 1)
                nc.vector.tensor_copy(prm_b[:, :, :], ps_s[:, 0:64].rearrange("p (a b) -> p a b", b=CT)).then_inc(s_prm, 1)
                dve.wait_ge(s_prm_t, 2)
                nc.vector.tensor_copy(prm_c[:, :, :], ps_s[:, BANK:BANK + 72].rearrange("p (a b) -> p a b", b=CT)).then_inc(s_prm, 1)
                dve.wait_ge(s_prm, 2)
                seq(nc.vector.memset(wf[:, :, HEADS:2 * HEADS].bitcast(mybir.dt.uint32), 0))
                seq(nc.vector.tensor_scalar(sp[:, 2, :], prm_c[:, C_LAM, :], -1.0, None, ALU.mult))
                seq(nc.vector.tensor_tensor(sp[:, 1, :], sp[:, 2, :], prm_c[:, C_LAM, :], ALU.max))
                for s in range(TT + 3):
                    if s < TT:
                        dve.wait_ge(s_ss, s + 1)
                        nc.vector.tensor_scalar(st8[:, 1, s:s + 1], st8[:, 0, s:s + 1], 1.0 / D, EPS, ALU.mult, ALU.add).then_inc(s_var, 1)
                    if 1 <= s <= TT:
                        dve.wait_ge(s_std, s)
                        nc.vector.reciprocal(st8[:, 3, s - 1:s], st8[:, 2, s - 1:s]).then_inc(s_rstd, 1)
                    if 2 <= s < TT + 2:
                        t = s - 2
                        dve.wait_ge(s_xt, t + 1)
                        if t >= 2:
                            dve.wait_ge(s_hlo, t - 1)
                        nc.vector.tensor_tensor(h_sb[t % 2][:, :].rearrange("p (k c) -> p k c", c=P),
                                                pair[t % 2][:, :].rearrange("p (k c) -> p k c", c=P),
                                                prm_c[:, C_PRE, :].unsqueeze(2).to_broadcast([P, KT, P]), ALU.mult).then_inc(s_hw, 1)
                    if s >= 3:
                        t = s - 3
                        dve.wait_ge(s_hhi, t + 1)
                        dve.wait_ge(s_hw, t + 1)
                        nc.vector.tensor_tensor(r1_lo[:, :, t * P:(t + 1) * P],
                                                h_sb[t % 2][:, :].rearrange("p (k c) -> p k c", c=P),
                                                r1_hi[:, :, t * P:(t + 1) * P].bitcast(f32), ALU.subtract).then_inc(s_hlo, 1)
                dve.wait_ge(s_wf_in, 32)
                seq(nc.vector.memset(ones_f, 1.0))
                nc.vector.memset(half[:, 0:1], 0.0).then_inc(s_wf, 1)
                dve.wait_ge(s_wf, 2)
                nc.vector.tensor_tensor(wf[:, :, 2 * HEADS:3 * HEADS], wf_raw[:, :, :],
                                        wf[:, :, 0:HEADS].bitcast(f32), ALU.subtract).then_inc(s_wf, 1)
                for j in range(2):
                    dve.wait_ge(s_whi, j + 1)
                    nc.vector.tensor_tensor(w_lo[:, j, :, :], raw[:, j, :].rearrange("p (k c) -> p k c", c=P),
                                            w_hi[:, j, :, :].bitcast(f32), ALU.subtract).then_inc(s_wlo, 1)
                dve.wait_ge(s_sp, 1)
                seq(nc.vector.tensor_scalar(sp[:, 1, :], sp[:, 0, :], 2.0, None, ALU.add))
                seq(nc.vector.reciprocal(sp[:, 3, :], sp[:, 1, :]))
                seq(nc.vector.tensor_tensor(sp[:, 1, :], sp[:, 0, :], sp[:, 3, :], ALU.mult))
                seq(nc.vector.tensor_tensor(sp[:, 3, :], sp[:, 1, :], sp[:, 1, :], ALU.mult))
                seq(nc.vector.tensor_scalar(sp[:, 4, :], sp[:, 3, :], 1.0 / 17, 1.0 / 15, ALU.mult, ALU.add))
                for k in (13, 11, 9, 7, 5, 3, 1):
                    seq(nc.vector.tensor_tensor(sp[:, 4, :], sp[:, 4, :], sp[:, 3, :], ALU.mult))
                    seq(nc.vector.tensor_scalar(sp[:, 4, :], sp[:, 4, :], 1.0 / k, None, ALU.add))
                seq(nc.vector.tensor_tensor(sp[:, 4, :], sp[:, 4, :], sp[:, 1, :], ALU.mult))
                seq(nc.vector.tensor_scalar(sp[:, 2, :], sp[:, 2, :], 0.0, None, ALU.max))
                seq(nc.vector.scalar_tensor_tensor(sp[:, 3, :], sp[:, 4, :], 2.0, sp[:, 2, :], ALU.mult, ALU.add))
                seq(nc.vector.tensor_scalar(rgk[:, 0, :], sp[:, 3, :], -RG_C, None, ALU.mult))
                seq(nc.vector.tensor_scalar(rgk[:, 1, :], sp[:, 3, :], RG_C / 2, None, ALU.mult))
                dve.wait_ge(s_fact, 1)
                nc.vector.scalar_tensor_tensor(f_a, ps_a[0:HEADS, :], bf[:, 0:1], f_lo, ALU.add, ALU.add).then_inc(s_f, 1)
                dve.wait_ge(s_f, 1)
                dve.sem_inc(s_sigr, 1)
                dve.wait_ge(s_fact, 2)
                seq(nc.vector.tensor_scalar(f_a, f_a, 0.0, None, ALU.min))
                dve.wait_ge(s_fact, 4)
                seq(nc.vector.tensor_tensor(f_a, f_a, f_l, ALU.subtract))
                seq(nc.vector.tensor_tensor_scan(f_c, ones_f, f_a, 0.0, ALU.mult, ALU.add))
                nc.vector.tensor_scalar(f_c, f_c, -1.0 / SCALE, None, ALU.mult).then_inc(s_c, 1)

                with dve.Fori(0, CT) as i:

                    def split_lo(r):
                        dve.wait_ge(s_whi, i * JOBS + (r + 1))
                        nc.vector.tensor_tensor(w_lo[:, r % 2, :, :], raw[:, r % 2, :].rearrange("p (k c) -> p k c", c=P),
                                                w_hi[:, r % 2, :, :].bitcast(f32), ALU.subtract).then_inc(s_wlo, 1)

                    def lo_rows(dst, src, hi, row, h):
                        rows = slice(h * HD, (h + 1) * HD)
                        to = slice((1 - h) * HD, (2 - h) * HD) if dst is q_st else rows
                        return nc.vector.scalar_tensor_tensor(dst[to, h, :], src[rows, :], prm_b[rows, row, bass.ds(i, 1)],
                                                              hi[rows, h, :].bitcast(f32), ALU.add, ALU.subtract)

                    tap = lambda j: prm_c[:, C_TAP + j, bass.ds(i, 1)]

                    def conv(j):
                        if j == 0:
                            dve.wait_ge(s_xr, i + 1)
                            nc.vector.tensor_scalar(xc[:, :], xpad[:, 0:SEQ], tap(0), prm_c[:, C_CB, bass.ds(i, 1)],
                                                    ALU.mult, ALU.add).then_inc(s_conv, 1)
                        else:
                            dve.wait_ge(s_conv, i * 4 + j)
                            nc.vector.scalar_tensor_tensor(xc[:, :], xpad[:, j:j + SEQ], tap(j), xc[:, :],
                                                           ALU.mult, ALU.add).then_inc(s_conv, 1)

                    for j in range(4):
                        conv(j)
                    split_lo(2)
                    for h in range(2):
                        dve.wait_ge(s_khi, i * 2 + (h + 1))
                        lo_rows(k_lo, ps_a, k_hi, B_K, h).then_inc(s_klo, 1)
                    split_lo(3)
                    for h in range(2):
                        dve.wait_ge(s_qhi, i * 2 + (h + 1))
                        lo_rows(q_st, ps_b, q_st, B_Q, h).then_inc(s_qlo, 1)
                    split_lo(4)
                    dve.wait_ge(s_sq, i + 1)
                    dve.wait_ge(s_a, i + 1)
                    nc.vector.scalar_tensor_tensor(s_tl[:, :], a_t[:, :], 1.0, s_tl[:, :], ALU.add, ALU.mult).then_inc(s_rg, 1)
                    dve.wait_ge(s_rg, i * 3 + 1)
                    dve.wait_ge(s_ix, i + 1)
                    nc.vector.tensor_tensor(s_tl[:, :], s_tl[:, :], i_t[:, :], ALU.mult).then_inc(s_rg, 1)
                    dve.wait_ge(s_rg, i * 3 + 2)
                    nc.vector.tensor_tensor_scan(r_t[:, :], a_t[:, :], s_tl[:, :], 0.0, ALU.mult, ALU.add).then_inc(s_rg, 1)
                    split_lo(5)

                    for s in range(STEPS + 1):
                        for c in range(2):
                            u = s - LAG
                            qb = u % QB
                            if 0 <= u < UNITS and (c == 0 or qb >= 4):
                                b0, b1 = 4 * c, min(4 * c + 4, qb + 1)
                                cols = slice((qb % 2) * P, (qb % 2 + 1) * P)
                                dve.wait_ge(s_phi, i * CHUNKS + (chunks_before(u) + c + 1))
                                nc.vector.tensor_tensor(pt_lo[:, b0:b1, cols],
                                                        ps_t[:, 0:(b1 - b0) * P].rearrange("p (b c) -> p b c", c=P),
                                                        pt_hi[:, b0:b1, cols].bitcast(f32), ALU.subtract).then_inc(s_plo, 1)
                            u = s - 2
                            if c == 0 and 0 <= u < UNITS:
                                n = (u % QB + 1) * P
                                dve.wait_ge(s_exp, i * UNITS + (u + 1))
                                nc.vector.reciprocal(rinv[:, u:u + 1], rs[:, u:u + 1]).then_inc(s_rinv, 1)
                                dve.wait_ge(s_rinv, i * UNITS + (u + 1))
                                nc.vector.tensor_scalar(probs[:, u % 3, 0:n], probs[:, u % 3, 0:n], rinv[:, u:u + 1], None,
                                                        ALU.mult).then_inc(s_norm, 1)
                        if s < UNITS:
                            n = (s % QB + 1) * P
                            if s == 0:
                                dve.wait_ge(s_cb, i * 32 + 32)
                            dve.wait_ge(s_s, i * UNITS + (s + 1))
                            dve.sem_inc(s_carry_v, 1)
                            nc.vector.tensor_tensor_reduce(probs[:, s % 3, 0:n], ps_s[:, 0:n], cb[:, s // QB, 0:n],
                                                           1.0, -3.0e38, ALU.add, ALU.max, mx[:, s:s + 1]).then_inc(s_max, 1)
                            dve.wait_ge(s_max, i * UNITS + (s + 2))
                            nc.vector.tensor_scalar(ngm[:, s:s + 1], mx[:, s:s + 1], -SCALE, None, ALU.mult).then_inc(s_neg, 1)
                        if s == 1:
                            dve.wait_ge(s_vhi, i + 1)
                            nc.vector.tensor_tensor(v_st[:, :, :, HD:P], ps_a[:, :].rearrange("p (k h c) -> p k h c", h=2, c=HD),
                                                    v_st[:, :, :, 0:HD].bitcast(f32), ALU.subtract).then_inc(s_vlo, 1)
                        for job in ("GA", "GR", "MA"):
                            if s == READ[job] + 1:
                                split_lo({"GA": 6, "GR": 7, "MA": 8}[job])
                        if 4 <= s < STEPS and s % 2 == 0:
                            g = (s - 4) // 2
                            rows = slice(0, HD) if g < QB // 2 else slice(HD, P)
                            q0 = (g % (QB // 2)) * 2 * P
                            if g == 0:
                                dve.wait_ge(s_stored, i + 1)
                            dve.wait_ge(s_pvc, i * QB + (g + 1))
                            nc.vector.tensor_tensor(y_t[rows, q0:q0 + 2 * P], ps_o[rows, 0:2 * P], half[rows, :],
                                                    ALU.add).then_inc(s_pva, 1)
                    split_lo(9)

            @block.tensor
            def _(pe):
                pe.wait_ge(s_const, 8)
                pe.wait_ge(s_prm_in, 8 * 16)
                nc.tensor.transpose(ps_s[:, 0:64], prm_in_b[:, :], ident[0:64, 0:64]).then_inc(s_prm_t, 1)
                nc.tensor.transpose(ps_s[:, BANK:BANK + 72], prm_in[:, :], ident[0:72, 0:72]).then_inc(s_prm_t, 1)
                for t in range(TT):
                    pe.wait_ge(s_xn, t + 1)
                    if t >= 2:
                        pe.wait_ge(s_hw, t - 1)
                    for k in range(KT):
                        last = nc.tensor.transpose(pair[t % 2][:, k * P:(k + 1) * P], x_sb[t][:, k * P:(k + 1) * P], ident[:, :])
                    last.then_inc(s_xt, 1)
                pe.wait_ge(s_hlo, TT)
                pe.wait_ge(s_wf, 3)
                for n in range(4 * KT):
                    kt, part = divmod(n, 4)
                    b = part % 2
                    last = nc.tensor.matmul(ps_a[0:3 * HEADS, b * BANK:(b + 1) * BANK], wf[:, kt, :],
                                            (r1_hi if part < 2 else r1_lo)[:, kt, b * BANK:(b + 1) * BANK],
                                            start=(kt == 0 and part < 2), stop=(kt == KT - 1 and part >= 2))
                last.then_inc(a_full, 1)

                with pe.Fori(0, CT) as i:

                    def weights(r):
                        pe.wait_ge(s_whi, i * JOBS + (r + 1))
                        pe.wait_ge(s_wlo, i * JOBS + (r + 3))

                    free = {"GA": (s_qlo, i * 2 + 2), "GR": (s_vlo, i + 1), "MA": (s_gaz, i + 1), "MR": (s_grz, i + 1)}

                    def filler(name, n):
                        job = {"GA": J_GA, "GR": J_GR, "MA": J_MA, "MR": J_MR}[name]
                        if n == 0:
                            pe.wait_ge(*free[name])
                            weights(job)
                        mm = project(pe, job % 2, pair[1 - job % 2], n, n + 1)
                        if n == MM - 1:
                            mm.then_inc(b_full if job % 2 == 0 else a_full, 1)

                    def gate(g, banks):
                        for b, dst in enumerate(banks):
                            mm = nc.tensor.matmul(dst, gw[:, g, :], xc[:, b * BANK:(b + 1) * BANK], start=True, stop=True)
                        mm.then_inc(s_gp, 1)

                    def transposes(u, c):
                        qb = u % QB
                        if not 0 <= u < UNITS or (c == 1 and qb < 4):
                            return
                        b0, b1 = 4 * c, min(4 * c + 4, qb + 1)
                        pe.wait_ge(s_norm, i * UNITS + (u + 1))
                        pe.wait_ge(s_plo, i * CHUNKS + (chunks_before(u) + c + 1))
                        for b in range(b0, b1):
                            last = nc.tensor.transpose(ps_t[:, (b - b0) * P:(b - b0 + 1) * P],
                                                       probs[:, u % 3, b * P:(b + 1) * P], ident[:, :])
                        last.then_inc(s_t, 1)

                    def scores(u):
                        h, qb = divmod(u, QB)
                        if u == 0:
                            pe.wait_ge(s_kdup, (i + 1) * 64)
                            pe.wait_ge(s_ri, i * 3 + 4)
                            pe.wait_ge(s_qlo, i * 2 + 2)
                        pe.wait_ge(s_max, i * UNITS + (u + 1))
                        for b in range(1 + (qb >= 4)):
                            n0, n1 = b * BANK, min((b + 1) * BANK, (qb + 1) * P)
                            diag = n1 == (qb + 1) * P
                            w = q_st[:, h, qb * P:(qb + 1) * P]
                            nc.tensor.matmul(ps_s[:, n0:n1], w, k_hi[:, h, n0:n1], start=True, stop=False)
                            last = nc.tensor.matmul(ps_s[:, n0:n1], w, k_lo[:, h, n0:n1], start=False, stop=not diag)
                            if diag:
                                last = nc.tensor.matmul(ps_s[:, n1 - P:n1], ident_b[:, :], mask_b[:, :],
                                                        start=False, stop=True)
                        last.then_inc(s_s, 1)

                    pe.wait_ge(s_maz, i + 1)
                    weights(J_XR)
                    project(pe, J_XR % 2, ps_b, 0, MM).then_inc(b_full, 1)
                    pe.wait_ge(s_sigr, i + 1)
                    weights(J_K)
                    project(pe, J_K % 2, ps_a, 0, MM).then_inc(a_full, 1)
                    pe.wait_ge(s_conv, i * 4 + 4)
                    pe.wait_ge(s_gw, (i + 1) * 64)
                    pe.wait_ge(s_max, i * UNITS + 1)
                    gate(0, (ps_s[:, 0:BANK], ps_s[:, BANK:2 * BANK]))
                    pe.wait_ge(s_plo, i * CHUNKS + 1)
                    pe.wait_ge(s_pva, i * QB + 1)
                    gate(1, (ps_t[:, :], ps_o[:, :]))
                    pe.wait_ge(s_xr, i + 1)
                    weights(J_Q)
                    project(pe, J_Q % 2, ps_b, 0, MM).then_inc(b_full, 1)
                    pe.wait_ge(s_klo, i * 2 + 2)
                    weights(J_V)
                    project(pe, J_V % 2, ps_a, 0, MM).then_inc(a_full, 1)

                    for s in range(STEPS):
                        transposes(s - LAG, 0)
                        for name, n in PLAN[2 * s]:
                            filler(name, n)
                        if s < UNITS:
                            scores(s)
                        transposes(s - LAG, 1)
                        for name, n in PLAN[2 * s + 1]:
                            filler(name, n)
                        if s == 0:
                            pe.wait_ge(s_v, i + 1)
                            for b in range(QB):
                                last = nc.tensor.transpose(ps_a[:, b * P:(b + 1) * P], stage[:, b * P:(b + 1) * P], ident[:, :])
                            last.then_inc(a_full, 1)
                        if s >= 4 and s % 2 == 0:
                            g = (s - 4) // 2
                            h, gq = divmod(g, QB // 2)
                            pe.wait_ge(s_plo, i * CHUNKS + (chunks_before(2 * g + 2) + 1))
                            pe.wait_ge(s_pva, i * QB + (g + 1))
                            if g == 0:
                                pe.wait_ge(s_vlo, i + 1)
                            blocks = 2 * gq + 2
                            for kb in range(blocks):
                                c0 = P if kb == blocks - 1 else 0
                                for pt in (pt_hi, pt_lo):
                                    last = nc.tensor.matmul(ps_o[:, c0:2 * P], v_st[:, kb, h, :], pt[:, kb, c0:2 * P],
                                                            start=(kb == 0 and pt is pt_hi),
                                                            stop=(kb == blocks - 1 and pt is pt_lo))
                            last.then_inc(s_pv, 1)

        one.close()
        r2_hi = sb("r2_hi", [P, KT, SEQ], f32r)
        r2_lo = sb("r2_lo", [P, KT, SEQ], f32r)
        m_t = sb("m_t", [P, CT, SEQ])
        two = sb("two", [P, 2, SEQ])
        tmp = sb("tmp", [P, SEQ])
        wo_raw = sb("wo_raw", [P, D])
        so = sb("so", [P, 4, TT])
        u_in = [sem(f"u_a_in_{k}") for k in range(KT)]
        ur_in = [sem("u_r_in_even"), sem("u_r_in_odd")]
        s_uhi, s_ulo, s_urhi, s_urlo = sem("u_a_hi"), sem("u_a_lo"), sem("u_r_hi"), sem("u_r_lo")
        sg_in = [sem("sig_in_even"), sem("sig_in_odd")]
        s_full, s_m, s_mr = sem("branch_full"), sem("m_ready"), sem("m_step")
        wo_in, s_wohi, s_wolo = sem("w_out_in"), sem("w_out_hi"), sem("w_out_lo")
        x_in = [sem("xres_in_even"), sem("xres_in_odd")]
        pw_in, s_mhi, s_mlo, s_o = sem("post_w_in"), sem("m_hi"), sem("m_lo"), sem("out_full")
        s_oss, s_ostd, s_orstd, s_onorm, s_oadd, s_oout, s_ostored = (sem(n) for n in (
            "out_sumsq", "out_std", "out_rstd", "out_scaled", "out_ready", "out_dma", "out_stored"))
        A0 = CT * JOBS
        R0 = A0 + CT
        A_FULLS = CT

        with nc.Block() as block:

            @block.sync
            def _(sp_):
                sp_.sem_inc(s_m, 2)
                sp_.sem_inc(s_onorm, 2)
                sp_.sem_inc(s_oadd, 2)
                sp_.sem_inc(s_ostored, 2)
                sp_.sem_inc(s_wolo, 1)
                sp_.sem_inc(s_urlo, 2)
                for k in range(0, KT, 2):
                    sp_.dma_start(r2_lo[:, k, :].bitcast(f32), ua_d[k]).then_inc(u_in[k], 16)
                with sp_.Fori(1, CT // 2) as j:
                    d = j * 2
                    for e in range(2):
                        sp_.wait_ge(s_wlo, A0 + d + (e + 1))
                        sp_.dma_start(raw[:, e, :].rearrange("p (k c) -> p k c", c=P),
                                      w_a_v[:, :, bass.ds(d * P + e * P, P)]).then_inc(raw_in[e], 16)
                with sp_.Fori(0, CT // 2) as j:
                    d = j * 2
                    for e in range(2):
                        sp_.wait_ge(s_wlo, R0 + d + (e + 1))
                        sp_.dma_start(raw[:, e, :].rearrange("p (k c) -> p k c", c=P),
                                      w_r_v[:, :, bass.ds(d * P + e * P, P)]).then_inc(raw_in[e], 16)
                sp_.wait_ge(s_m, 2 * CT + 2)
                with sp_.Fori(0, TT // 2) as j:
                    t = j * 2
                    for e in range(2):
                        sp_.wait_ge(s_oadd, t + (e + 1))
                        sp_.dma_start(two[:, e, :], x_v[bass.ds(t + e, 1)].rearrange("o p c -> (o p) c")).then_inc(x_in[e], 16)

            @block.gpsimd
            def _(pool):
                for e in range(2):
                    pool.dma_start(two[:, e, :], sig_d[e]).then_inc(sg_in[e], 16)
                with pool.Fori(0, KT // 2) as j:
                    for e in range(2):
                        pool.wait_ge(s_urlo, j * 2 + (e + 1))
                        pool.sem_inc(s_carry, 1)
                        pool.dma_start(r1_lo[:, bass.ds(j * 2 + e, 1), :].rearrange("p o c -> p (o c)").bitcast(f32),
                                       ur_d[bass.ds(j * 2 + e, 1)].rearrange("o p c -> (o p) c")).then_inc(ur_in[e], 16)
                        pool.wait_ge(s_m, j * 2 + (e + 3))
                        pool.sem_inc(s_carry, 1)
                        pool.dma_start(two[:, e, :], sig_d[bass.ds(j * 2 + (e + 2), 1)].rearrange("o p c -> (o p) c")).then_inc(sg_in[e], 16)
                with pool.Fori(0, CT // 2 - 1) as j:
                    for e in range(2):
                        pool.wait_ge(s_m, j * 2 + (CT + e + 3))
                        pool.sem_inc(s_carry, 1)
                        pool.dma_start(two[:, e, :], sig_d[bass.ds(j * 2 + (CT + e + 2), 1)].rearrange("o p c -> (o p) c")).then_inc(sg_in[e], 16)
                with pool.Fori(0, TT // 2) as j:
                    t = j * 2
                    for e in range(2):
                        pool.wait_ge(s_onorm, t + (e + 3))
                        pool.wait_ge(x_in[e], t * 8 + 16)
                        nc.gpsimd.tensor_tensor(raw[:, e, :], raw[:, e, :], two[:, e, :], ALU.add).then_inc(s_oadd, 1)
                        pool.wait_ge(s_oadd, t + (e + 3))
                        pool.sem_inc(s_carry, 1)
                        pool.dma_start(out_v[bass.ds(t + e, 1)].rearrange("o p c -> (o p) c"), raw[:, e, :]).then_inc(s_oout, 16)
                        pool.wait_ge(s_oout, t * 16 + (16 * e + 16))
                        pool.sem_inc(s_ostored, 1)

            @block.scalar
            def _(act):
                for k in range(1, KT, 2):
                    act.dma_start(r2_lo[:, k, :].bitcast(f32), ua_d[k]).then_inc(u_in[k], 16)
                act.dma_start(wo_raw[:, :], w_out_v[0]).then_inc(wo_in, 16)
                for k in range(KT):
                    act.wait_ge(u_in[k], 16)
                    nc.scalar.activation(r2_hi[:, k, :], r2_lo[:, k, :].bitcast(f32), ACT.Copy).then_inc(s_uhi, 1)

                def split_hi(count, e):
                    act.wait_ge(raw_in[e], count)
                    nc.scalar.activation(w_hi[:, e, :, :], raw[:, e, :].rearrange("p (k c) -> p k c", c=P), ACT.Copy).then_inc(s_whi, 1)

                with act.Fori(0, CT // 2) as j:
                    d = j * 2
                    for e in range(2):
                        act.wait_ge(s_full, d + (e + 1))
                        split_hi(d * 8 + (A0 * 8 + 32), e)
                        act.wait_ge(ur_in[e], d * 8 + 16)
                        row = lambda z: z[:, bass.ds(d + e, 1), :].rearrange("p o c -> p (o c)")
                        nc.scalar.activation(row(r1_hi), row(r1_lo).bitcast(f32), ACT.Copy).then_inc(s_urhi, 1)

                def branch_r(d, e, more):
                    act.wait_ge(wo_in, (d + e) * 16 + 16)
                    nc.scalar.activation(r2_hi[:, d + e, :] if isinstance(d, int) else r2_hi[:, bass.ds(d + e, 1), :].rearrange("p o c -> p (o c)"),
                                         wo_raw[:, :], ACT.Copy).then_inc(s_wohi, 1)
                    act.wait_ge(s_full, d + (CT + e + 1))
                    if more:
                        split_hi(d * 8 + (R0 * 8 + 32), e)
                    if more or e == 0:
                        act.wait_ge(s_wolo, d + (e + 2))
                        act.dma_start(wo_raw[:, :], w_out_v[d + e + 1] if isinstance(d, int)
                                      else w_out_v[bass.ds(d + (e + 1), 1)].rearrange("o p c -> (o p) c")).then_inc(wo_in, 16)

                with act.Fori(0, (CT - 2) // 2) as j:
                    d = j * 2
                    for e in range(2):
                        branch_r(d, e, True)
                for e in range(2):
                    branch_r(CT - 2, e, False)
                act.wait_ge(s_wolo, CT + 1)
                act.dma_start(wo_raw[:, :], post_w[0:1, :].to_broadcast([P, D])).then_inc(pw_in, 16)

                def m_hi(t, e):
                    nc.scalar.activation(r1_hi[:, e, :].rearrange("p (k c) -> p k c", c=P),
                                         m_t[:, :, bass.ds(t * P + e * P, P)], ACT.Copy).then_inc(s_mhi, 1)

                def out_stats(t, e):
                    act.wait_ge(s_o, t + (e + 1))
                    nc.scalar.activation(tmp[:, :], pair[e][:, :], ACT.Square,
                                         accum_out=so[:, 0, bass.ds(t + e, 1)]).then_inc(s_oss, 1)
                    act.wait_ge(s_oss, 2 * t + (2 * e + 2))
                    nc.scalar.activation(so[:, 2, bass.ds(t + e, 1)], so[:, 1, bass.ds(t + e, 1)], ACT.Sqrt).then_inc(s_ostd, 1)

                act.wait_ge(s_m, 2 * CT + 2)
                m_hi(0, 0)
                m_hi(0, 1)
                with act.Fori(0, (TT - 2) // 2) as j:
                    t = j * 2
                    for e in range(2):
                        out_stats(t, e)
                        m_hi(t + 2, e)
                for e in range(2):
                    out_stats(TT - 2, e)

            @block.vector
            def _(dve):
                def split_lo(count, e):
                    dve.wait_ge(s_whi, count)
                    nc.vector.tensor_tensor(w_lo[:, e, :, :], raw[:, e, :].rearrange("p (k c) -> p k c", c=P),
                                            w_hi[:, e, :, :].bitcast(f32), ALU.subtract).then_inc(s_wlo, 1)

                for k in range(KT):
                    dve.wait_ge(s_uhi, k + 1)
                    nc.vector.tensor_tensor(r2_lo[:, k, :], r2_lo[:, k, :].bitcast(f32), r2_hi[:, k, :].bitcast(f32),
                                            ALU.subtract).then_inc(s_ulo, 1)
                with dve.Fori(0, CT // 2) as j:
                    d = j * 2
                    for e in range(2):
                        dve.wait_ge(s_full, d + (e + 1))
                        dve.wait_ge(sg_in[e], d * 8 + 16)
                        nc.vector.tensor_tensor(m_t[:, bass.ds(d + e, 1), :].rearrange("p o c -> p (o c)"), pair[e][:, :],
                                                two[:, e, :], ALU.mult).then_inc(s_m, 1)
                        split_lo(d + (A0 + e + 3), e)
                        dve.wait_ge(s_urhi, d + (e + 1))
                        row = lambda z: z[:, bass.ds(d + e, 1), :].rearrange("p o c -> p (o c)")
                        nc.vector.tensor_tensor(row(r1_lo), row(r1_lo).bitcast(f32), row(r1_hi).bitcast(f32),
                                                ALU.subtract).then_inc(s_urlo, 1)

                def branch_r(d, e, more):
                    dve.wait_ge(s_wohi, d + (e + 1))
                    row = lambda z: z[:, bass.ds(d + e, 1), :].rearrange("p o c -> p (o c)")
                    nc.vector.tensor_tensor(row(r2_lo), wo_raw[:, :], row(r2_hi).bitcast(f32), ALU.subtract).then_inc(s_wolo, 1)
                    dve.wait_ge(s_full, d + (CT + e + 1))
                    dve.wait_ge(sg_in[e], d * 8 + (CT * 8 + 16))
                    dve.wait_ge(s_m, d + (CT + e + 2))
                    nc.vector.tensor_tensor(tmp[:, :], pair[e][:, :], two[:, e, :], ALU.mult).then_inc(s_mr, 1)
                    dve.wait_ge(s_mr, d + (e + 1))
                    nc.vector.tensor_tensor(row(m_t), row(m_t), tmp[:, :], ALU.add).then_inc(s_m, 1)
                    if more:
                        split_lo(d + (R0 + e + 3), e)

                with dve.Fori(0, (CT - 2) // 2) as j:
                    d = j * 2
                    for e in range(2):
                        branch_r(d, e, True)
                for e in range(2):
                    branch_r(CT - 2, e, False)

                def m_lo(t, e):
                    dve.wait_ge(s_mhi, t + (e + 1))
                    nc.vector.tensor_tensor(r1_lo[:, e, :].rearrange("p (k c) -> p k c", c=P),
                                            m_t[:, :, bass.ds(t * P + e * P, P)],
                                            r1_hi[:, e, :].rearrange("p (k c) -> p k c", c=P).bitcast(f32),
                                            ALU.subtract).then_inc(s_mlo, 1)

                def finish(t, e):
                    c = lambda k: so[:, k, bass.ds(t + e, 1)]
                    dve.wait_ge(s_oss, 2 * t + (2 * e + 1))
                    nc.vector.tensor_scalar(c(1), c(0), 1.0 / D, EPS, ALU.mult, ALU.add).then_inc(s_oss, 1)
                    dve.wait_ge(s_ostd, t + (e + 1))
                    nc.vector.reciprocal(c(3), c(2)).then_inc(s_orstd, 1)
                    dve.wait_ge(s_orstd, t + (e + 1))
                    dve.wait_ge(s_ostored, t + (e + 1))
                    nc.vector.scalar_tensor_tensor(raw[:, e, :], pair[e][:, :], c(3), wo_raw[:, :],
                                                   ALU.mult, ALU.mult).then_inc(s_onorm, 1)

                dve.wait_ge(s_m, 2 * CT + 2)
                m_lo(0, 0)
                m_lo(0, 1)
                dve.wait_ge(pw_in, 16)
                with dve.Fori(0, (TT - 2) // 2) as j:
                    t = j * 2
                    for e in range(2):
                        finish(t, e)
                        m_lo(t + 2, e)
                for e in range(2):
                    finish(TT - 2, e)

            @block.tensor
            def _(pe):
                def rank(e, kt, hi, lo):
                    for part in range(6):
                        w = (w_hi if part < 4 else w_lo)[:, e, kt, :]
                        u = lo if part in (2, 3) else hi
                        cols = slice((part % 2) * BANK, (part % 2 + 1) * BANK)
                        last = nc.tensor.matmul(pair[e][:, cols], w, u[:, kt, cols],
                                                start=(kt == 0 and part < 2), stop=(kt == KT - 1 and part >= 4))
                    return last

                def branch(d, e, n, hi, lo):
                    pe.wait_ge(s_whi, d + ((A0, R0)[n] + e + 1))
                    pe.wait_ge(s_wlo, d + ((A0, R0)[n] + e + 3))
                    pe.wait_ge(s_m, d + (n * CT + e + 1))
                    for kt in range(KT):
                        last = rank(e, kt, hi, lo)
                    last.then_inc(s_full, 1)

                for e in range(2):
                    pe.wait_ge(s_whi, A0 + e + 1)
                    pe.wait_ge(s_wlo, A0 + e + 3)
                for kt in range(KT):
                    pe.wait_ge(s_ulo, kt + 1)
                    for e in range(2):
                        last = rank(e, kt, r2_hi, r2_lo)
                        if kt == KT - 1:
                            last.then_inc(s_full, 1)
                with pe.Fori(1, CT // 2) as j:
                    d = j * 2
                    for e in range(2):
                        branch(d, e, 0, r2_hi, r2_lo)
                pe.wait_ge(s_urlo, KT + 2)
                with pe.Fori(0, CT // 2) as j:
                    d = j * 2
                    for e in range(2):
                        branch(d, e, 1, r1_hi, r1_lo)
                pe.wait_ge(s_wolo, CT + 1)
                with pe.Fori(0, TT // 2) as j:
                    t = j * 2
                    for e in range(2):
                        pe.wait_ge(s_mlo, t + (e + 1))
                        pe.wait_ge(s_onorm, t + (e + 1))
                        for kt in range(KT):
                            for part in range(6):
                                m = (r1_hi if part < 4 else r1_lo)[:, e, kt * P:(kt + 1) * P]
                                w = r2_lo if part in (2, 3) else r2_hi
                                cols = slice((part % 2) * BANK, (part % 2 + 1) * BANK)
                                last = nc.tensor.matmul(pair[e][:, cols], m, w[:, kt, cols],
                                                        start=(kt == 0 and part < 2), stop=(kt == KT - 1 and part >= 4))
                        last.then_inc(s_o, 1)


_INS = ["x", "pre_norm_w", "w_in", "b_in", "conv_w", "conv_b", "rg_wa", "rg_ba", "rg_wx", "rg_bx",
        "rg_lambda", "w_branch_a", "w_branch_r", "w_out", "post_norm_w"]


def kernel(**inputs):
    import numpy as _np
    import concourse.bacc as _bacc
    from concourse import mybir as _mybir
    from concourse.bass_utils import run_bass_kernel_spmd as _run

    nc = _bacc.Bacc("TRN2", target_bir_lowering=False, num_devices=1)
    arrays, args = {}, []
    for name in _INS:
        a = _np.ascontiguousarray(inputs[name])
        arrays[f"in_{name}"] = a
        args.append(nc.dram_tensor(f"in_{name}", a.shape, _mybir.dt.from_np(a.dtype), kind="ExternalInput").ap())
    args.append(nc.dram_tensor("out_0", (1, SEQ, D), _mybir.dt.float32, kind="ExternalOutput").ap())
    build(nc, *args)
    r = _run(nc, [arrays], core_ids=[0])
    return r.results[0]["out_0"]
```

```python
import concourse.bass as bass
from concourse import mybir
from contextlib import ExitStack

P = 128
D = 1024
SEQ = 1024
KT = D // P
TT = SEQ // P
CT = D // P
HD = 64
HEADS = D // HD
QB = SEQ // P
UNITS = 2 * QB
BANK = 512
EPS = 1e-6
RG_C = 8.0
MASK = -1e30
SCALE = HD ** -0.5

Q_COL, K_COL, V_COL, F_COL = 0, D, 2 * D, 3 * D
GA_COL = 3 * D + HEADS
XR_COL, GR_COL, MA_COL, MR_COL = (GA_COL + n * D for n in (1, 2, 3, 4))
JOB_COLS = [XR_COL, K_COL, Q_COL, V_COL, GA_COL, GR_COL, MA_COL, MR_COL]
J_XR, J_K, J_Q, J_V, J_GA, J_GR, J_MA, J_MR = range(8)
JOBS = 8
B_Q, B_K, B_V, B_GA, B_XR, B_GR, B_MA, B_MR = range(8)
C_TAP, C_CB, C_BA, C_BX, C_LAM, C_PRE = 0, 4, 5, 6, 7, 8

MM = 6 * KT
A_K, A_V, A_VT, A_GR, A_MR, FILLS_A = 1, 2, 3, 4, 5, 5
B_XR_, B_Q_, B_GA_, B_MA_, FILLS_B = 1, 2, 3, 4, 4
CHUNKS = 2 * sum(1 + (b >= 4) for b in range(QB))
LAG = 3
STEPS = UNITS + LAG


def chunks_before(u):
    return sum(1 + (v % QB >= 4) for v in range(u))


def filler_plan():
    seq = [(name, n) for name in ("GA", "GR", "MA", "MR") for n in range(MM)]
    share = []
    for s in range(STEPS):
        two = s >= LAG and (s - LAG) % QB >= 4
        share += [8 if two and s >= UNITS else 5 if two else 4, 7 if two and s % 2 == 0 else 5]
    total = sum(share)
    plan, read, at = [], {}, 0
    for s in range(2 * STEPS):
        part = []
        while at < len(seq) and at * total < len(seq) * sum(share[:s + 1]):
            part.append(seq[at])
            read[seq[at][0]] = (s + 1) // 2
            at += 1
        plan.append(part)
    return plan, read


PLAN, READ = filler_plan()


def build(nc, x, pre_w, w_in, b_in, conv_w, conv_b, rg_wa, rg_ba, rg_wx, rg_bx, lam, w_a, w_r,
          w_out, post_w, out):
    f32, f32r, bf16 = mybir.dt.float32, mybir.dt.float32r, mybir.dt.bfloat16
    ACT, ALU = mybir.ActivationFunctionType, mybir.AluOpType

    w_in_v = w_in[0].rearrange("(k p) c -> p k c", p=P)
    w_a_v = w_a[0].rearrange("(k p) c -> p k c", p=P)
    w_r_v = w_r[0].rearrange("(k p) c -> p k c", p=P)
    w_out_v = w_out[0].rearrange("(k p) c -> k p c", p=P)
    x_v = x[0].rearrange("(t p) d -> t p d", p=P)
    out_v = out[0].rearrange("(t p) d -> t p d", p=P)

    ua_d, ur_d = (nc.dram_tensor(f"{n}_scratch", (CT, P, SEQ), f32, kind="Internal").ap() for n in ("u_a", "u_r"))
    sig_d = nc.dram_tensor("merge_gate_scratch", (2 * CT, P, SEQ), f32, kind="Internal").ap()
    c_d = nc.dram_tensor("c_scratch", (HEADS, SEQ), f32, kind="Internal").ap()

    ctx = ExitStack()
    with ctx:
        def sb(name, shape, dt=f32, stack=ctx):
            return stack.enter_context(nc.sbuf_tensor(name, shape, dt))

        def sem(name):
            return ctx.enter_context(nc.semaphore(name))

        r1_hi = sb("r1_hi", [P, KT, SEQ], f32r)
        r1_lo = sb("r1_lo", [P, KT, SEQ], f32r)
        raw = sb("raw", [P, 2, KT * P])
        w_hi = sb("w_hi", [P, 2, KT, P], f32r)
        w_lo = sb("w_lo", [P, 2, KT, P], f32r)
        ring = sb("ring", [P, KT, SEQ], f32r)
        two = sb("two", [P, 2, SEQ])
        y_t = sb("y_t", [P, SEQ])
        ident = sb("ident", [P, P])
        ident_b = sb("ident_b", [P, P], bf16)
        mask_b = sb("mask_b", [P, P], bf16)
        prm_b = sb("prm_b", [P, 8, CT])
        prm_c = sb("prm_c", [P, 9, CT])
        rgk = sb("rgk", [P, 2, CT])

        ps_a = ctx.enter_context(nc.psum_tensor("ps_a", [P, 2 * BANK], f32))
        ps_b = ctx.enter_context(nc.psum_tensor("ps_b", [P, 2 * BANK], f32))
        ps_s = ctx.enter_context(nc.psum_tensor("ps_s", [P, 2 * BANK], f32))
        ps_t = ctx.enter_context(nc.psum_tensor("ps_t", [P, BANK], f32))
        ps_o = ctx.enter_context(nc.psum_tensor("ps_o", [P, BANK], f32))
        pair = [ps_a, ps_b]

        raw_in = [sem("raw_in_even"), sem("raw_in_odd")]
        s_whi, s_wlo = sem("w_hi_ready"), sem("w_lo_ready")
        s_carry, s_carry_v, s_carry_s = (sem(f"wait_carrier_{e}") for e in ("pool", "vector", "sync"))
        s_const, s_prm_in, s_prm_t, s_prm = sem("consts"), sem("params_in"), sem("params_t"), sem("params")
        s_x = [sem(f"x_in_{t}") for t in range(TT)]
        s_ss, s_var, s_std, s_rstd, s_xn = sem("sumsq"), sem("mean_square"), sem("std"), sem("rstd"), sem("x_scaled")
        s_xt, s_hw, s_hhi, s_hlo = sem("x_transposed"), sem("h_weighted"), sem("h_hi"), sem("h_lo")
        s_pro = sem("dve_prologue_step")
        s_wf_in, s_wf, s_f, s_fact, s_c = (sem(n) for n in ("wf_in", "wf_split", "f_summed", "f_act", "c_ready"))
        s_sp = sem("softplus_act")
        a_full, b_full = sem("pair_a_full"), sem("pair_b_full")
        s_qhi, s_qlo, s_khi, s_klo, s_kdup, s_v, s_vhi, s_vlo = (sem(n) for n in (
            "q_hi", "q_lo", "k_hi", "k_lo", "k_dup", "v_sb", "v_hi", "v_lo"))
        s_s, s_max, s_neg, s_exp = sem("scores_ready"), sem("row_max"), sem("neg_max"), sem("exp_done")
        s_rinv, s_norm = sem("row_sum_inv"), sem("probs_ready")
        s_t, s_phi, s_plo = sem("probs_t"), sem("p_hi"), sem("p_lo")
        s_pv, s_pvc, s_pva = sem("values_ready"), sem("values_half"), sem("values_added")
        s_cb = sem("c_broadcast_in")
        s_xr, s_conv, s_gw = sem("xr_padded"), sem("conv_step"), sem("gate_weights_in")
        s_ri, s_tanh, s_sq, s_a = sem("r_i_ready"), sem("tanh_ready"), sem("sqrt_ready"), sem("decay_ready")
        s_gp = sem("gate_products")
        s_ix, s_rg = sem("i_times_x"), sem("rg_step")
        s_gaz, s_grz, s_maz = sem("gate_a_linear"), sem("gate_r_linear"), sem("merge_a_linear")
        s_ga, s_gr, s_sig, s_sigr = sem("gate_a_ready"), sem("gate_r_ready"), sem("merge_a_ready"), sem("merge_r_ready")
        s_ur, s_ua, s_out, s_urout = sem("ur_ready"), sem("ua_ready"), sem("results_stored"), sem("ur_stored")
        s_c_out = sem("c_stored")
        u_in = [sem(f"u_a_in_{k}") for k in range(KT)]
        s_stored = sem("iteration_stored")

        one = ExitStack()
        pt_hi = sb("pt_hi", [P, QB, 2 * P], f32r, one)
        pt_lo = sb("pt_lo", [P, QB, 2 * P], f32r, one)
        q_st = ring[:, 0:2, :]
        k_hi = ring[:, 2:4, :]
        k_lo = ring[:, 4:6, :]
        v_st = ring[:, 6:8, :].rearrange("p a (b h c) -> p (a b) h c", h=2, c=P)
        AHEAD = 4
        FREE = 6
        probs = sb("probs", [P, 3, SEQ], f32, one)
        cb = sb("cb", [P, 2, SEQ], f32, one)
        stage, gate_m = two[:, 0, :], two[:, 1, :]
        gate_a = sb("gate_a", [P, SEQ], f32, one)
        half = sb("half", [P, 2 * P], f32, one)
        PAD = 3
        xpad = sb("xpad", [P, PAD + SEQ], f32, one)
        xc = sb("xc", [P, SEQ], f32, one)
        r_t = sb("r_t", [P, SEQ], f32, one)
        i_t = sb("i_t", [P, SEQ], f32, one)
        a_t = sb("a_t", [P, SEQ], f32, one)
        s_tl = sb("s_tl", [P, SEQ], f32, one)
        gw = sb("gw", [P, 2, P], f32, one)
        mx = sb("mx", [P, UNITS], f32, one)
        ngm = sb("ngm", [P, UNITS], f32, one)
        rs = sb("rs", [P, UNITS], f32, one)
        rinv = sb("rinv", [P, UNITS], f32, one)
        st8 = sb("st8", [P, 4, TT], f32, one)
        wf_raw = sb("wf_raw", [P, KT, HEADS], f32, one)
        wf = sb("wf", [P, KT, 3 * HEADS], f32r, one)
        bf = sb("bf", [HEADS, 1], f32, one)
        sp = sb("sp", [P, 5, CT], f32, one)
        prm_in = sb("prm_in", [72, P], f32, one)
        prm_in_b = sb("prm_in_b", [64, P], f32, one)
        x_sb = [probs[:, 0, :], probs[:, 1, :], probs[:, 2, :], i_t[:, :], a_t[:, :], s_tl[:, :], gate_a[:, :], y_t[:, :]]
        h_sb = [stage, xc[:, :]]
        f_lo, f_a, f_b, f_l, f_c = (z[0:HEADS, :] for z in (xc, i_t, a_t, s_tl, r_t))
        ones_f = y_t[0:HEADS, :]

        def project(pe, slot, dst, first, last):
            for n in range(first, last):
                kt, part = divmod(n, 6)
                w = (w_hi if part < 4 else w_lo)[:, slot, kt, :]
                h = r1_lo if part in (2, 3) else r1_hi
                b = part % 2
                mm = nc.tensor.matmul(dst[:, b * BANK:(b + 1) * BANK], w,
                                      h[:, kt, b * BANK:(b + 1) * BANK],
                                      start=(kt == 0 and part < 2), stop=(kt == KT - 1 and part >= 4))
            return mm

        with nc.Block() as block:

            @block.sync
            def _(sp_):
                for s in (s_max, s_maz, s_ur, s_ri, s_pva, s_plo):
                    sp_.sem_inc(s, 1)
                sp_.sem_inc(s_wlo, 2)
                sp_.sem_inc(s_out, 16)
                sp_.dma_start(x_sb[0], x_v[0]).then_inc(s_x[0], 16)
                sp_.dma_start(prm_in_b[0:24, :], b_in[0, 0:3 * D].rearrange("(r c) -> r c", c=P)).then_inc(s_prm_in, 16)
                sp_.dma_start(prm_in_b[24:64, :], b_in[0, GA_COL:GA_COL + 5 * D].rearrange("(r c) -> r c", c=P)).then_inc(s_prm_in, 16)
                sp_.dma_start(prm_in[0:32, :], conv_w[0].rearrange("j (r c) -> (j r) c", c=P)).then_inc(s_prm_in, 16)
                for n, v in enumerate((conv_b, rg_ba, rg_bx, lam, pre_w)):
                    sp_.dma_start(prm_in[32 + 8 * n:40 + 8 * n, :], v[0].rearrange("(r c) -> r c", c=P)).then_inc(s_prm_in, 16)
                for t in range(2, TT, 2):
                    sp_.dma_start(x_sb[t], x_v[t]).then_inc(s_x[t], 16)
                sp_.dma_start(wf_raw[:, :, :], w_in_v[:, :, F_COL:F_COL + HEADS]).then_inc(s_wf_in, 16)
                sp_.dma_start(bf[:, :], b_in[0, F_COL:F_COL + HEADS].rearrange("(h o) -> h o", o=1)).then_inc(s_wf_in, 16)
                with sp_.Fori(0, CT) as i:
                    for r in range(JOBS):
                        src = w_in_v[:, :, bass.ds(i * P + JOB_COLS[r], P)]
                        sp_.wait_ge(s_wlo, i * JOBS + (r + 1))
                        sp_.sem_inc(s_carry_s, 1)
                        sp_.dma_start(raw[:, r % 2, :].rearrange("p (k c) -> p k c", c=P), src).then_inc(raw_in[r % 2], 16)

                for r in range(2):
                    sp_.wait_ge(s_wlo, CT * JOBS + (r + 1))
                    sp_.dma_start(raw[:, r, :].rearrange("p (k c) -> p k c", c=P),
                                  w_a_v[:, :, r * P:(r + 1) * P]).then_inc(raw_in[r], 16)
                sp_.wait_ge(s_stored, CT)
                sp_.wait_ge(s_s, CT * UNITS)
                for k in range(FREE):
                    sp_.dma_start(ring[:, k, :].bitcast(f32), ua_d[k]).then_inc(u_in[k], 16)

            @block.gpsimd
            def _(pool):
                nc.gpsimd.memset(ident[:, :], 0.0).then_inc(s_const, 1)
                nc.gpsimd.memset(ident_b[:, :], 0.0).then_inc(s_const, 1)
                nc.gpsimd.memset(mask_b[:, :], 0.0).then_inc(s_const, 1)
                pool.wait_ge(s_const, 3)
                for m in (ident, ident_b):
                    nc.gpsimd.affine_select(out=m[:, :], in_=m[:, :], compare_op=ALU.not_equal, fill=1.0,
                                            base=0, pattern=[[-1, P]], channel_multiplier=1).then_inc(s_const, 1)
                nc.gpsimd.affine_select(out=mask_b[:, :], in_=mask_b[:, :], compare_op=ALU.is_ge, fill=MASK,
                                        base=0, pattern=[[-1, P]], channel_multiplier=1).then_inc(s_const, 1)
                nc.gpsimd.memset(gw[:, :, :], 0.0).then_inc(s_const, 1)
                nc.gpsimd.memset(xpad[:, 0:PAD], 0.0).then_inc(s_const, 1)
                pool.wait_ge(s_const, 8)
                for t in range(TT):
                    pool.wait_ge(s_rstd, t + 1)
                    nc.gpsimd.tensor_tensor(x_sb[t], x_sb[t], st8[:, 3, t:t + 1].to_broadcast([P, SEQ]), ALU.mult).then_inc(s_xn, 1)
                pool.wait_ge(s_c, 1)
                pool.dma_start(c_d, f_c).then_inc(s_c_out, 16)
                pool.wait_ge(s_c_out, 16)
                with pool.Fori(0, CT) as i:
                    pool.wait_ge(s_out, i * 48 + 16)
                    pool.sem_inc(s_stored, 1)
                    pool.wait_ge(s_max, i * UNITS + 1)
                    pool.sem_inc(s_carry, 1)
                    for h in range(2):
                        pool.dma_start(cb[:, h, :], c_d[bass.ds(i * 2 + h, 1), :].to_broadcast([P, SEQ])).then_inc(s_cb, 16)
                    pool.wait_ge(s_ri, i * 3 + 1)
                    pool.sem_inc(s_carry, 1)
                    for g, w in enumerate((rg_wa, rg_wx)):
                        for b in range(2):
                            pool.dma_start(gw[b * HD:(b + 1) * HD, g, b * HD:(b + 1) * HD],
                                           w[0, bass.ds(i * 2 + b, 1), :, :].rearrange("o a b -> (o a) b")).then_inc(s_gw, 16)
                    pool.wait_ge(s_klo, i * 2 + 2)
                    pool.sem_inc(s_carry, 1)
                    for t in (k_hi, k_lo):
                        pool.dma_start(t[HD:P, 0, :].bitcast(f32), t[0:HD, 0, :].bitcast(f32)).then_inc(s_kdup, 16)
                        pool.dma_start(t[0:HD, 1, :].bitcast(f32), t[HD:P, 1, :].bitcast(f32)).then_inc(s_kdup, 16)
                    pool.wait_ge(s_ri, i * 3 + 4)
                    pool.wait_ge(s_conv, i * 4 + 4)
                    nc.gpsimd.tensor_tensor(i_t[:, :], i_t[:, :], xc[:, :], ALU.mult).then_inc(s_ix, 1)
                    pool.wait_ge(s_gr, i + 1)
                    pool.wait_ge(s_rg, i * 3 + 3)
                    nc.gpsimd.tensor_tensor(r_t[:, :], r_t[:, :], xpad[:, PAD:], ALU.mult).then_inc(s_ur, 1)
                    pool.wait_ge(s_ur, i + 2)
                    pool.sem_inc(s_carry, 1)
                    pool.dma_start(ur_d[bass.ds(i, 1)].rearrange("o p c -> (o p) c"), r_t[:, :]).then_inc(s_urout, 16)
                    pool.wait_ge(s_urout, i * 16 + 16)

            @block.scalar
            def _(act):
                for t in range(1, TT, 2):
                    act.dma_start(x_sb[t], x_v[t]).then_inc(s_x[t], 16)
                for s in range(TT + AHEAD):
                    if s < TT:
                        act.wait_ge(s_x[s], 16)
                        if s:
                            act.wait_ge(s_ss, s)
                        nc.scalar.activation(r_t[:, :], x_sb[s], ACT.Square, accum_out=st8[:, 0, s:s + 1]).then_inc(s_ss, 1)
                    if 1 <= s <= TT:
                        t = s - 1
                        act.wait_ge(s_var, t + 1)
                        nc.scalar.activation(st8[:, 2, t:t + 1], st8[:, 1, t:t + 1], ACT.Sqrt).then_inc(s_std, 1)
                    if s == 2:
                        act.wait_ge(s_wf_in, 32)
                        act.wait_ge(s_wf, 1)
                        nc.scalar.activation(wf[:, :, 0:HEADS], wf_raw[:, :, :], ACT.Copy).then_inc(s_wf, 1)
                    if s >= AHEAD:
                        t = s - AHEAD
                        act.wait_ge(s_hw, t + 1)
                        nc.scalar.activation(r1_hi[:, :, t * P:(t + 1) * P],
                                             h_sb[t % 2].rearrange("p (k c) -> p k c", c=P), ACT.Copy).then_inc(s_hhi, 1)
                for j in range(2):
                    act.wait_ge(raw_in[j], 16)
                    nc.scalar.activation(w_hi[:, j, :, :], raw[:, j, :].rearrange("p (k c) -> p k c", c=P), ACT.Copy).then_inc(s_whi, 1)
                act.wait_ge(s_pro, 2)
                nc.scalar.activation(sp[:, 0, :], sp[:, 1, :], ACT.Exp, scale=-1.0).then_inc(s_sp, 1)
                act.wait_ge(a_full, 1)
                nc.scalar.activation(f_lo, ps_a[2 * HEADS:3 * HEADS, :], ACT.Identity).then_inc(s_fact, 1)
                act.wait_ge(s_f, 1)
                nc.scalar.activation(f_b, f_a, ACT.Abs).then_inc(s_fact, 1)
                act.wait_ge(s_fact, 2)
                nc.scalar.activation(f_b, f_b, ACT.Exp, scale=-1.0).then_inc(s_fact, 1)
                act.wait_ge(s_fact, 3)
                nc.scalar.activation(f_l, f_b, ACT.Ln, bias=1.0).then_inc(s_fact, 1)

                with act.Fori(0, CT) as i:

                    def split_hi(r):
                        act.wait_ge(raw_in[r % 2], i * (JOBS * 8) + 16 * (r // 2 + 1))
                        nc.scalar.activation(w_hi[:, r % 2, :, :], raw[:, r % 2, :].rearrange("p (k c) -> p k c", c=P),
                                             ACT.Copy).then_inc(s_whi, 1)

                    bias = lambda row: prm_b[:, row, bass.ds(i, 1)]
                    bias_c = lambda row: prm_c[:, row, bass.ds(i, 1)]
                    act.wait_ge(b_full, i * FILLS_B + B_XR_)
                    act.wait_ge(s_ur, i + 1)
                    nc.scalar.activation(xpad[:, PAD:], ps_b[:, :], ACT.Identity, bias=bias(B_XR)).then_inc(s_xr, 1)
                    split_hi(2)
                    act.wait_ge(a_full, i * FILLS_A + (A_K + 1))
                    for h in range(2):
                        rows = slice(h * HD, (h + 1) * HD)
                        nc.scalar.activation(k_hi[rows, h, :], ps_a[rows, :], ACT.Identity,
                                             bias=prm_b[rows, B_K, bass.ds(i, 1)]).then_inc(s_khi, 1)
                    split_hi(3)
                    act.wait_ge(s_gp, i * 2 + 1)
                    act.wait_ge(s_stored, i + 1)
                    nc.scalar.activation(r_t[:, :], ps_s[:, :], ACT.Sigmoid, bias=bias_c(C_BA)).then_inc(s_ri, 1)
                    act.wait_ge(s_gp, i * 2 + 2)
                    for b, ps in enumerate((ps_t, ps_o)):
                        nc.scalar.activation(i_t[:, b * BANK:(b + 1) * BANK], ps[:, :], ACT.Sigmoid, bias=bias_c(C_BX)).then_inc(s_ri, 1)
                    act.wait_ge(s_ri, i * 3 + 2)
                    nc.scalar.activation(s_tl[:, :], r_t[:, :], ACT.Tanh, scale=rgk[:, 1, bass.ds(i, 1)]).then_inc(s_tanh, 1)
                    act.wait_ge(b_full, i * FILLS_B + B_Q_)
                    for h in range(2):
                        rows = slice(h * HD, (h + 1) * HD)
                        nc.scalar.activation(q_st[rows, h, :], ps_b[rows, :], ACT.Identity,
                                             bias=prm_b[rows, B_Q, bass.ds(i, 1)]).then_inc(s_qhi, 1)
                    split_hi(4)
                    act.wait_ge(s_tanh, i + 1)
                    nc.scalar.activation(s_tl[:, :], s_tl[:, :], ACT.Sqrt).then_inc(s_sq, 1)
                    nc.scalar.activation(a_t[:, :], r_t[:, :], ACT.Exp, scale=rgk[:, 0, bass.ds(i, 1)]).then_inc(s_a, 1)
                    act.wait_ge(a_full, i * FILLS_A + (A_V + 1))
                    nc.scalar.activation(stage, ps_a[:, :], ACT.Identity, bias=bias(B_V)).then_inc(s_v, 1)
                    split_hi(5)

                    for s in range(STEPS + 1):
                        for c in range(2):
                            u = s - LAG
                            qb = u % QB
                            if 0 <= u < UNITS and (c == 0 or qb >= 4):
                                b0, b1 = 4 * c, min(4 * c + 4, qb + 1)
                                act.wait_ge(s_t, i * CHUNKS + (chunks_before(u) + c + 1))
                                nc.scalar.activation(pt_hi[:, b0:b1, (qb % 2) * P:(qb % 2 + 1) * P],
                                                     ps_t[:, 0:(b1 - b0) * P].rearrange("p (b c) -> p b c", c=P),
                                                     ACT.Copy).then_inc(s_phi, 1)
                            u = s - 1
                            if c == 0 and 0 <= u < UNITS:
                                n = (u % QB + 1) * P
                                act.wait_ge(s_neg, i * UNITS + (u + 1))
                                nc.scalar.activation(probs[:, u % 3, 0:n], probs[:, u % 3, 0:n], ACT.Exp, scale=SCALE,
                                                     bias=ngm[:, u:u + 1], accum_out=rs[:, u:u + 1]).then_inc(s_exp, 1)
                        if s == 1:
                            act.wait_ge(a_full, i * FILLS_A + (A_VT + 1))
                            nc.scalar.activation(v_st[:, :, :, 0:HD],
                                                 ps_a[:, :].rearrange("p (k h c) -> p k h c", h=2, c=HD), ACT.Copy).then_inc(s_vhi, 1)
                        if s == READ["GA"]:
                            act.wait_ge(b_full, i * FILLS_B + B_GA_)
                            nc.scalar.activation(gate_a[:, :], ps_b[:, :], ACT.Identity, bias=bias(B_GA)).then_inc(s_gaz, 1)
                        if s == READ["GA"] + 1:
                            split_hi(6)
                        if s == READ["GR"]:
                            act.wait_ge(a_full, i * FILLS_A + (A_GR + 1))
                            act.wait_ge(s_conv, i * 4 + 4)
                            nc.scalar.activation(xpad[:, PAD:], ps_a[:, :], ACT.Identity, bias=bias(B_GR)).then_inc(s_grz, 1)
                        if s == READ["GR"] + 1:
                            split_hi(7)
                        if s == READ["MA"]:
                            act.wait_ge(b_full, i * FILLS_B + B_MA_)
                            nc.scalar.activation(stage, ps_b[:, :], ACT.Identity, bias=bias(B_MA)).then_inc(s_maz, 1)
                        if s == READ["MA"] + 1:
                            split_hi(8)
                        if s == UNITS:
                            act.wait_ge(s_grz, i + 1)
                            nc.scalar.activation(xpad[:, PAD:], xpad[:, PAD:], ACT.Silu).then_inc(s_gr, 1)
                        if s == UNITS + 1:
                            act.wait_ge(s_gaz, i + 1)
                            nc.scalar.activation(gate_a[:, :], gate_a[:, :], ACT.Silu).then_inc(s_ga, 1)
                        if s == UNITS + 2:
                            act.wait_ge(s_maz, i + 2)
                            nc.scalar.activation(stage, stage, ACT.Sigmoid).then_inc(s_sig, 1)
                        if 4 <= s < STEPS and s % 2 == 0:
                            g = (s - 4) // 2
                            mine, other = (slice(0, HD), slice(HD, P)) if g < QB // 2 else (slice(HD, P), slice(0, HD))
                            act.wait_ge(s_pv, i * QB + (g + 1))
                            nc.scalar.activation(half[mine, :], ps_o[other, 0:2 * P], ACT.Copy).then_inc(s_pvc, 1)
                        if s == STEPS:
                            split_hi(9)
                            act.wait_ge(a_full, i * FILLS_A + (A_MR + 1))
                            nc.scalar.activation(gate_m, ps_a[:, :], ACT.Sigmoid, bias=bias(B_MR)).then_inc(s_sigr, 1)
                    rows = lambda z, n=0: z[bass.ds(i + n, 1)].rearrange("o p c -> (o p) c")
                    sig_rows_a, u_rows, sig_rows_r = rows(sig_d), rows(ua_d), rows(sig_d, CT)
                    act.wait_ge(s_sig, i + 1)
                    act.dma_start(sig_rows_a, stage).then_inc(s_out, 16)
                    act.wait_ge(s_ua, i + 1)
                    act.dma_start(u_rows, y_t[:, :]).then_inc(s_out, 16)
                    act.wait_ge(s_sigr, i + 2)
                    act.dma_start(sig_rows_r, gate_m).then_inc(s_out, 16)

            @block.vector
            def _(dve):
                pro = [0]

                def seq(ins):
                    pro[0] += 1
                    ins.then_inc(s_pro, 1)
                    dve.wait_ge(s_pro, pro[0])

                def params():
                    dve.wait_ge(s_prm_t, 1)
                    nc.vector.tensor_copy(prm_b[:, :, :], ps_s[:, 0:64].rearrange("p (a b) -> p a b", b=CT)).then_inc(s_prm, 1)
                    dve.wait_ge(s_prm_t, 2)
                    nc.vector.tensor_copy(prm_c[:, :, :], ps_s[:, BANK:BANK + 72].rearrange("p (a b) -> p a b", b=CT)).then_inc(s_prm, 1)
                    dve.wait_ge(s_prm, 2)
                    nc.vector.memset(wf[:, :, HEADS:2 * HEADS].bitcast(mybir.dt.uint32), 0).then_inc(s_wf, 1)
                    seq(nc.vector.tensor_scalar(sp[:, 2, :], prm_c[:, C_LAM, :], -1.0, None, ALU.mult))
                    seq(nc.vector.tensor_tensor(sp[:, 1, :], sp[:, 2, :], prm_c[:, C_LAM, :], ALU.max))

                for s in range(TT + AHEAD + 1):
                    if s < TT:
                        dve.wait_ge(s_ss, s + 1)
                        nc.vector.tensor_scalar(st8[:, 1, s:s + 1], st8[:, 0, s:s + 1], 1.0 / D, EPS, ALU.mult, ALU.add).then_inc(s_var, 1)
                    if 1 <= s <= TT:
                        dve.wait_ge(s_std, s)
                        nc.vector.reciprocal(st8[:, 3, s - 1:s], st8[:, 2, s - 1:s]).then_inc(s_rstd, 1)
                    if s == 1:
                        params()
                    if AHEAD <= s < TT + AHEAD:
                        t = s - AHEAD
                        dve.wait_ge(s_xt, t + 1)
                        if t >= 2:
                            dve.wait_ge(s_hlo, t - 1)
                        nc.vector.tensor_tensor(h_sb[t % 2].rearrange("p (k c) -> p k c", c=P),
                                                pair[t % 2][:, :].rearrange("p (k c) -> p k c", c=P),
                                                prm_c[:, C_PRE, :].unsqueeze(2).to_broadcast([P, KT, P]), ALU.mult).then_inc(s_hw, 1)
                    if s == 3:
                        dve.wait_ge(s_wf_in, 32)
                        dve.wait_ge(s_wf, 2)
                        nc.vector.tensor_tensor(wf[:, :, 2 * HEADS:3 * HEADS], wf_raw[:, :, :],
                                                wf[:, :, 0:HEADS].bitcast(f32), ALU.subtract).then_inc(s_wf, 1)
                    if s > AHEAD:
                        t = s - AHEAD - 1
                        dve.wait_ge(s_hhi, t + 1)
                        dve.wait_ge(s_hw, t + 1)
                        nc.vector.tensor_tensor(r1_lo[:, :, t * P:(t + 1) * P],
                                                h_sb[t % 2].rearrange("p (k c) -> p k c", c=P),
                                                r1_hi[:, :, t * P:(t + 1) * P].bitcast(f32), ALU.subtract).then_inc(s_hlo, 1)
                for j in range(2):
                    dve.wait_ge(s_whi, j + 1)
                    nc.vector.tensor_tensor(w_lo[:, j, :, :], raw[:, j, :].rearrange("p (k c) -> p k c", c=P),
                                            w_hi[:, j, :, :].bitcast(f32), ALU.subtract).then_inc(s_wlo, 1)
                dve.wait_ge(s_sp, 1)
                seq(nc.vector.tensor_scalar(sp[:, 1, :], sp[:, 0, :], 2.0, None, ALU.add))
                seq(nc.vector.reciprocal(sp[:, 3, :], sp[:, 1, :]))
                seq(nc.vector.tensor_tensor(sp[:, 1, :], sp[:, 0, :], sp[:, 3, :], ALU.mult))
                seq(nc.vector.tensor_tensor(sp[:, 3, :], sp[:, 1, :], sp[:, 1, :], ALU.mult))
                seq(nc.vector.tensor_scalar(sp[:, 4, :], sp[:, 3, :], 1.0 / 17, 1.0 / 15, ALU.mult, ALU.add))
                for k in (13, 11, 9, 7, 5, 3, 1):
                    seq(nc.vector.tensor_tensor(sp[:, 4, :], sp[:, 4, :], sp[:, 3, :], ALU.mult))
                    seq(nc.vector.tensor_scalar(sp[:, 4, :], sp[:, 4, :], 1.0 / k, None, ALU.add))
                seq(nc.vector.tensor_tensor(sp[:, 4, :], sp[:, 4, :], sp[:, 1, :], ALU.mult))
                seq(nc.vector.tensor_scalar(sp[:, 2, :], sp[:, 2, :], 0.0, None, ALU.max))
                seq(nc.vector.scalar_tensor_tensor(sp[:, 3, :], sp[:, 4, :], 2.0, sp[:, 2, :], ALU.mult, ALU.add))
                seq(nc.vector.tensor_scalar(rgk[:, 0, :], sp[:, 3, :], -RG_C, None, ALU.mult))
                seq(nc.vector.tensor_scalar(rgk[:, 1, :], sp[:, 3, :], RG_C / 2, None, ALU.mult))
                seq(nc.vector.memset(ones_f, 1.0))
                dve.wait_ge(s_fact, 1)
                nc.vector.scalar_tensor_tensor(f_a, ps_a[0:HEADS, :], bf[:, 0:1], f_lo, ALU.add, ALU.add).then_inc(s_f, 1)
                dve.wait_ge(s_f, 1)
                dve.sem_inc(s_sigr, 1)
                dve.wait_ge(s_fact, 2)
                seq(nc.vector.tensor_scalar(f_a, f_a, 0.0, None, ALU.min))
                dve.wait_ge(s_fact, 4)
                seq(nc.vector.tensor_tensor(f_a, f_a, f_l, ALU.subtract))
                seq(nc.vector.tensor_tensor_scan(f_c, ones_f, f_a, 0.0, ALU.mult, ALU.add))
                nc.vector.tensor_scalar(f_c, f_c, -1.0 / SCALE, None, ALU.mult).then_inc(s_c, 1)

                with dve.Fori(0, CT) as i:

                    def split_lo(r):
                        dve.wait_ge(s_whi, i * JOBS + (r + 1))
                        nc.vector.tensor_tensor(w_lo[:, r % 2, :, :], raw[:, r % 2, :].rearrange("p (k c) -> p k c", c=P),
                                                w_hi[:, r % 2, :, :].bitcast(f32), ALU.subtract).then_inc(s_wlo, 1)

                    def lo_rows(dst, src, hi, row, h, head_swap=False):
                        rows = slice(h * HD, (h + 1) * HD)
                        to = slice((1 - h) * HD, (2 - h) * HD) if head_swap else rows
                        return nc.vector.scalar_tensor_tensor(dst[to, h, :], src[rows, :], prm_b[rows, row, bass.ds(i, 1)],
                                                              hi[rows, h, :].bitcast(f32), ALU.add, ALU.subtract)

                    tap = lambda j: prm_c[:, C_TAP + j, bass.ds(i, 1)]

                    def conv(j):
                        if j == 0:
                            dve.wait_ge(s_xr, i + 1)
                            nc.vector.tensor_scalar(xc[:, :], xpad[:, 0:SEQ], tap(0), prm_c[:, C_CB, bass.ds(i, 1)],
                                                    ALU.mult, ALU.add).then_inc(s_conv, 1)
                        else:
                            dve.wait_ge(s_conv, i * 4 + j)
                            nc.vector.scalar_tensor_tensor(xc[:, :], xpad[:, j:j + SEQ], tap(j), xc[:, :],
                                                           ALU.mult, ALU.add).then_inc(s_conv, 1)

                    for j in range(4):
                        conv(j)
                    split_lo(2)
                    for h in range(2):
                        dve.wait_ge(s_khi, i * 2 + (h + 1))
                        lo_rows(k_lo, ps_a, k_hi, B_K, h).then_inc(s_klo, 1)
                    split_lo(3)
                    for h in range(2):
                        dve.wait_ge(s_qhi, i * 2 + (h + 1))
                        lo_rows(q_st, ps_b, q_st, B_Q, h, True).then_inc(s_qlo, 1)
                    split_lo(4)
                    dve.wait_ge(s_sq, i + 1)
                    dve.wait_ge(s_a, i + 1)
                    nc.vector.scalar_tensor_tensor(s_tl[:, :], a_t[:, :], 1.0, s_tl[:, :], ALU.add, ALU.mult).then_inc(s_rg, 1)
                    dve.wait_ge(s_rg, i * 3 + 1)
                    dve.wait_ge(s_ix, i + 1)
                    nc.vector.tensor_tensor(s_tl[:, :], s_tl[:, :], i_t[:, :], ALU.mult).then_inc(s_rg, 1)
                    dve.wait_ge(s_rg, i * 3 + 2)
                    nc.vector.tensor_tensor_scan(r_t[:, :], a_t[:, :], s_tl[:, :], 0.0, ALU.mult, ALU.add).then_inc(s_rg, 1)
                    split_lo(5)

                    for s in range(STEPS + 1):
                        for c in range(2):
                            u = s - LAG
                            qb = u % QB
                            if 0 <= u < UNITS and (c == 0 or qb >= 4):
                                b0, b1 = 4 * c, min(4 * c + 4, qb + 1)
                                cols = slice((qb % 2) * P, (qb % 2 + 1) * P)
                                dve.wait_ge(s_phi, i * CHUNKS + (chunks_before(u) + c + 1))
                                nc.vector.tensor_tensor(pt_lo[:, b0:b1, cols],
                                                        ps_t[:, 0:(b1 - b0) * P].rearrange("p (b c) -> p b c", c=P),
                                                        pt_hi[:, b0:b1, cols].bitcast(f32), ALU.subtract).then_inc(s_plo, 1)
                            u = s - 2
                            if c == 0 and 0 <= u < UNITS:
                                n = (u % QB + 1) * P
                                dve.wait_ge(s_exp, i * UNITS + (u + 1))
                                nc.vector.reciprocal(rinv[:, u:u + 1], rs[:, u:u + 1]).then_inc(s_rinv, 1)
                                dve.wait_ge(s_rinv, i * UNITS + (u + 1))
                                nc.vector.tensor_scalar(probs[:, u % 3, 0:n], probs[:, u % 3, 0:n], rinv[:, u:u + 1], None,
                                                        ALU.mult).then_inc(s_norm, 1)
                        if s < UNITS:
                            n = (s % QB + 1) * P
                            if s == 0:
                                dve.wait_ge(s_cb, i * 32 + 32)
                            dve.wait_ge(s_s, i * UNITS + (s + 1))
                            dve.sem_inc(s_carry_v, 1)
                            nc.vector.tensor_tensor_reduce(probs[:, s % 3, 0:n], ps_s[:, 0:n], cb[:, s // QB, 0:n],
                                                           1.0, -3.0e38, ALU.add, ALU.max, mx[:, s:s + 1]).then_inc(s_max, 1)
                            dve.wait_ge(s_max, i * UNITS + (s + 2))
                            nc.vector.tensor_scalar(ngm[:, s:s + 1], mx[:, s:s + 1], -SCALE, None, ALU.mult).then_inc(s_neg, 1)
                        if s == 1:
                            dve.wait_ge(s_vhi, i + 1)
                            nc.vector.tensor_tensor(v_st[:, :, :, HD:P], ps_a[:, :].rearrange("p (k h c) -> p k h c", h=2, c=HD),
                                                    v_st[:, :, :, 0:HD].bitcast(f32), ALU.subtract).then_inc(s_vlo, 1)
                        for job in ("GA", "GR", "MA"):
                            if s == READ[job] + 1:
                                split_lo({"GA": 6, "GR": 7, "MA": 8}[job])
                        if 4 <= s < STEPS and s % 2 == 0:
                            g = (s - 4) // 2
                            rows = slice(0, HD) if g < QB // 2 else slice(HD, P)
                            q0 = (g % (QB // 2)) * 2 * P
                            if g == 0:
                                dve.wait_ge(s_stored, i + 1)
                            dve.wait_ge(s_pvc, i * QB + (g + 1))
                            nc.vector.tensor_tensor(y_t[rows, q0:q0 + 2 * P], ps_o[rows, 0:2 * P], half[rows, :],
                                                    ALU.add).then_inc(s_pva, 1)
                    dve.wait_ge(s_pva, i * QB + (QB + 1))
                    dve.wait_ge(s_ga, i + 1)
                    nc.vector.tensor_tensor(y_t[:, :], y_t[:, :], gate_a[:, :], ALU.mult).then_inc(s_ua, 1)
                    split_lo(9)

            @block.tensor
            def _(pe):
                pe.wait_ge(s_const, 8)
                pe.wait_ge(s_prm_in, 8 * 16)
                nc.tensor.transpose(ps_s[:, 0:64], prm_in_b[:, :], ident[0:64, 0:64]).then_inc(s_prm_t, 1)
                nc.tensor.transpose(ps_s[:, BANK:BANK + 72], prm_in[:, :], ident[0:72, 0:72]).then_inc(s_prm_t, 1)
                for t in range(TT):
                    pe.wait_ge(s_xn, t + 1)
                    if t >= 2:
                        pe.wait_ge(s_hw, t - 1)
                    for k in range(KT):
                        last = nc.tensor.transpose(pair[t % 2][:, k * P:(k + 1) * P], x_sb[t][:, k * P:(k + 1) * P], ident[:, :])
                    last.then_inc(s_xt, 1)
                pe.wait_ge(s_wf, 3)
                for b in range(2):
                    pe.wait_ge(s_hlo, TT // 2 * (b + 1))
                    pe.wait_ge(s_hw, TT - 1)
                    for n in range(2 * KT):
                        kt, part = divmod(n, 2)
                        last = nc.tensor.matmul(ps_a[0:3 * HEADS, b * BANK:(b + 1) * BANK], wf[:, kt, :],
                                                (r1_hi if part == 0 else r1_lo)[:, kt, b * BANK:(b + 1) * BANK],
                                                start=(n == 0), stop=(n == 2 * KT - 1))
                last.then_inc(a_full, 1)

                with pe.Fori(0, CT) as i:

                    def weights(r):
                        pe.wait_ge(s_whi, i * JOBS + (r + 1))
                        pe.wait_ge(s_wlo, i * JOBS + (r + 3))

                    free = {"GA": (s_qlo, i * 2 + 2), "GR": (s_vlo, i + 1), "MA": (s_gaz, i + 1), "MR": (s_grz, i + 1)}

                    def filler(name, n):
                        job = {"GA": J_GA, "GR": J_GR, "MA": J_MA, "MR": J_MR}[name]
                        if n == 0:
                            pe.wait_ge(*free[name])
                            weights(job)
                        mm = project(pe, job % 2, pair[1 - job % 2], n, n + 1)
                        if n == MM - 1:
                            mm.then_inc(b_full if job % 2 == 0 else a_full, 1)

                    def gate(g, banks):
                        for b, dst in enumerate(banks):
                            mm = nc.tensor.matmul(dst, gw[:, g, :], xc[:, b * BANK:(b + 1) * BANK], start=True, stop=True)
                        mm.then_inc(s_gp, 1)

                    def transposes(u, c):
                        qb = u % QB
                        if not 0 <= u < UNITS or (c == 1 and qb < 4):
                            return
                        b0, b1 = 4 * c, min(4 * c + 4, qb + 1)
                        pe.wait_ge(s_norm, i * UNITS + (u + 1))
                        pe.wait_ge(s_plo, i * CHUNKS + (chunks_before(u) + c + 1))
                        for b in range(b0, b1):
                            last = nc.tensor.transpose(ps_t[:, (b - b0) * P:(b - b0 + 1) * P],
                                                       probs[:, u % 3, b * P:(b + 1) * P], ident[:, :])
                        last.then_inc(s_t, 1)

                    def scores(u):
                        h, qb = divmod(u, QB)
                        if u == 0:
                            pe.wait_ge(s_kdup, (i + 1) * 64)
                            pe.wait_ge(s_ri, i * 3 + 4)
                            pe.wait_ge(s_qlo, i * 2 + 2)
                        pe.wait_ge(s_max, i * UNITS + (u + 1))
                        for b in range(1 + (qb >= 4)):
                            n0, n1 = b * BANK, min((b + 1) * BANK, (qb + 1) * P)
                            diag = n1 == (qb + 1) * P
                            w = q_st[:, h, qb * P:(qb + 1) * P]
                            nc.tensor.matmul(ps_s[:, n0:n1], w, k_hi[:, h, n0:n1], start=True, stop=False)
                            last = nc.tensor.matmul(ps_s[:, n0:n1], w, k_lo[:, h, n0:n1], start=False, stop=not diag)
                            if diag:
                                last = nc.tensor.matmul(ps_s[:, n1 - P:n1], ident_b[:, :], mask_b[:, :],
                                                        start=False, stop=True)
                        last.then_inc(s_s, 1)

                    pe.wait_ge(s_maz, i + 1)
                    weights(J_XR)
                    project(pe, J_XR % 2, ps_b, 0, MM).then_inc(b_full, 1)
                    pe.wait_ge(s_sigr, i + 1)
                    weights(J_K)
                    project(pe, J_K % 2, ps_a, 0, MM).then_inc(a_full, 1)
                    pe.wait_ge(s_conv, i * 4 + 4)
                    pe.wait_ge(s_gw, (i + 1) * 64)
                    pe.wait_ge(s_max, i * UNITS + 1)
                    gate(0, (ps_s[:, 0:BANK], ps_s[:, BANK:2 * BANK]))
                    pe.wait_ge(s_plo, i * CHUNKS + 1)
                    pe.wait_ge(s_pva, i * QB + 1)
                    gate(1, (ps_t[:, :], ps_o[:, :]))
                    pe.wait_ge(s_xr, i + 1)
                    weights(J_Q)
                    project(pe, J_Q % 2, ps_b, 0, MM).then_inc(b_full, 1)
                    pe.wait_ge(s_klo, i * 2 + 2)
                    weights(J_V)
                    project(pe, J_V % 2, ps_a, 0, MM).then_inc(a_full, 1)

                    for s in range(STEPS):
                        transposes(s - LAG, 0)
                        for name, n in PLAN[2 * s]:
                            filler(name, n)
                        if s < UNITS:
                            scores(s)
                        transposes(s - LAG, 1)
                        for name, n in PLAN[2 * s + 1]:
                            filler(name, n)
                        if s == 0:
                            pe.wait_ge(s_v, i + 1)
                            for b in range(QB):
                                last = nc.tensor.transpose(ps_a[:, b * P:(b + 1) * P], stage[:, b * P:(b + 1) * P], ident[:, :])
                            last.then_inc(a_full, 1)
                        if s >= 4 and s % 2 == 0:
                            g = (s - 4) // 2
                            h, gq = divmod(g, QB // 2)
                            pe.wait_ge(s_plo, i * CHUNKS + (chunks_before(2 * g + 2) + 1))
                            pe.wait_ge(s_pva, i * QB + (g + 1))
                            if g == 0:
                                pe.wait_ge(s_vlo, i + 1)
                            blocks = 2 * gq + 2
                            for kb in range(blocks):
                                c0 = P if kb == blocks - 1 else 0
                                for pt in (pt_hi, pt_lo):
                                    last = nc.tensor.matmul(ps_o[:, c0:2 * P], v_st[:, kb, h, :], pt[:, kb, c0:2 * P],
                                                            start=(kb == 0 and pt is pt_hi),
                                                            stop=(kb == blocks - 1 and pt is pt_lo))
                            last.then_inc(s_pv, 1)

        one.close()
        r2_hi = sb("r2_hi", [P, KT, SEQ], f32r)
        r2_lo = ring
        m_t = sb("m_t", [P, CT, SEQ])
        tmp = y_t
        wo_raw = sb("wo_raw", [P, D])
        so = sb("so", [P, 4, TT])
        ur_in = [sem(f"u_r_in_{k}") for k in range(KT)]
        s_uhi, s_ulo, s_urhi, s_urlo = sem("u_a_hi"), sem("u_a_lo"), sem("u_r_hi"), sem("u_r_lo")
        sg_in = [sem("sig_in_even"), sem("sig_in_odd")]
        s_full, s_m, s_mr = sem("branch_full"), sem("m_ready"), sem("m_step")
        wo_in, s_wohi, s_wolo = sem("w_out_in"), sem("w_out_hi"), sem("w_out_lo")
        x_in = [sem("xres_in_even"), sem("xres_in_odd")]
        pw_in, s_mhi, s_mlo, s_o = sem("post_w_in"), sem("m_hi"), sem("m_lo"), sem("out_full")
        s_oss, s_ostd, s_orstd, s_onorm, s_oadd = (sem(n) for n in (
            "out_sumsq", "out_std", "out_rstd", "out_scaled", "out_ready"))
        s_oout = [sem("out_stored_even"), sem("out_stored_odd")]
        A0 = CT * JOBS
        R0 = A0 + CT

        with nc.Block() as block:

            @block.sync
            def _(sp_):
                sp_.sem_inc(s_m, 2)
                sp_.sem_inc(s_onorm, 2)
                for e in range(2):
                    sp_.sem_inc(s_oout[e], 16)
                sp_.sem_inc(s_wolo, 1)
                sp_.wait_ge(s_out, CT * 48 + 16)
                for k in range(FREE, KT):
                    sp_.dma_start(r2_lo[:, k, :].bitcast(f32), ua_d[k]).then_inc(u_in[k], 16)
                for k in range(KT // 2):
                    sp_.dma_start(r1_lo[:, k, :].bitcast(f32), ur_d[k]).then_inc(ur_in[k], 16)
                for e in range(2):
                    sp_.wait_ge(s_wlo, A0 + 2 + (e + 1))
                    sp_.dma_start(raw[:, e, :].rearrange("p (k c) -> p k c", c=P),
                                  w_a_v[:, :, (e + 2) * P:(e + 3) * P]).then_inc(raw_in[e], 16)
                for k in range(KT // 2, KT):
                    sp_.dma_start(r1_lo[:, k, :].bitcast(f32), ur_d[k]).then_inc(ur_in[k], 16)
                with sp_.Fori(2, CT // 2) as j:
                    d = j * 2
                    for e in range(2):
                        sp_.wait_ge(s_wlo, A0 + d + (e + 1))
                        sp_.dma_start(raw[:, e, :].rearrange("p (k c) -> p k c", c=P),
                                      w_a_v[:, :, bass.ds(d * P + e * P, P)]).then_inc(raw_in[e], 16)
                with sp_.Fori(0, CT // 2) as j:
                    d = j * 2
                    for e in range(2):
                        sp_.wait_ge(s_wlo, R0 + d + (e + 1))
                        sp_.dma_start(raw[:, e, :].rearrange("p (k c) -> p k c", c=P),
                                      w_r_v[:, :, bass.ds(d * P + e * P, P)]).then_inc(raw_in[e], 16)
                sp_.wait_ge(s_m, 2 * CT + 2)
                for e in range(2):
                    sp_.dma_start(two[:, e, :], x_v[e]).then_inc(x_in[e], 16)
                with sp_.Fori(0, (TT - 2) // 2) as j:
                    t = j * 2
                    for e in range(2):
                        out_rows, x_rows = out_v[bass.ds(t + e, 1)], x_v[bass.ds(t + (e + 2), 1)]
                        sp_.wait_ge(s_oadd, t + (e + 1))
                        sp_.sem_inc(s_carry_s, 1)
                        sp_.dma_start(out_rows.rearrange("o p c -> (o p) c"), raw[:, e, :]).then_inc(s_oout[e], 16)
                        sp_.dma_start(two[:, e, :], x_rows.rearrange("o p c -> (o p) c")).then_inc(x_in[e], 16)
                for e in range(2):
                    sp_.wait_ge(s_oadd, TT - 1 + e)
                    sp_.dma_start(out_v[TT - 2 + e], raw[:, e, :]).then_inc(s_oout[e], 16)
                for e in range(2):
                    sp_.wait_ge(s_oout[e], TT // 2 * 16 + 16)

            @block.gpsimd
            def _(pool):
                pool.wait_ge(s_out, CT * 48 + 16)
                for e in range(2):
                    pool.dma_start(two[:, e, :], sig_d[e]).then_inc(sg_in[e], 16)
                with pool.Fori(0, CT - 1) as j:
                    for e in range(2):
                        pool.wait_ge(s_m, j * 2 + (e + 3))
                        pool.sem_inc(s_carry, 1)
                        pool.dma_start(two[:, e, :], sig_d[bass.ds(j * 2 + (e + 2), 1)].rearrange("o p c -> (o p) c")).then_inc(sg_in[e], 16)

            @block.scalar
            def _(act):
                act.dma_start(wo_raw[:, :], w_out_v[0]).then_inc(wo_in, 16)
                for k in range(KT):
                    act.wait_ge(u_in[k], 16)
                    nc.scalar.activation(r2_hi[:, k, :], r2_lo[:, k, :].bitcast(f32), ACT.Copy).then_inc(s_uhi, 1)

                def split_hi(count, e):
                    act.wait_ge(raw_in[e], count)
                    nc.scalar.activation(w_hi[:, e, :, :], raw[:, e, :].rearrange("p (k c) -> p k c", c=P), ACT.Copy).then_inc(s_whi, 1)

                def split_ur_hi(k):
                    act.wait_ge(ur_in[k], 16)
                    nc.scalar.activation(r1_hi[:, k, :], r1_lo[:, k, :].bitcast(f32), ACT.Copy).then_inc(s_urhi, 1)

                for k in range(KT // 2):
                    split_ur_hi(k)
                for e in range(2):
                    act.wait_ge(s_full, e + 1)
                    split_hi(A0 * 8 + 32, e)
                for k in range(KT // 2, KT):
                    split_ur_hi(k)
                with act.Fori(1, CT // 2) as j:
                    d = j * 2
                    for e in range(2):
                        act.wait_ge(s_full, d + (e + 1))
                        split_hi(d * 8 + (A0 * 8 + 32), e)

                def branch_r(d, e, more):
                    act.wait_ge(wo_in, (d + e) * 16 + 16)
                    nc.scalar.activation(r2_hi[:, d + e, :] if isinstance(d, int) else r2_hi[:, bass.ds(d + e, 1), :].rearrange("p o c -> p (o c)"),
                                         wo_raw[:, :], ACT.Copy).then_inc(s_wohi, 1)
                    act.wait_ge(s_full, d + (CT + e + 1))
                    if more:
                        split_hi(d * 8 + (R0 * 8 + 32), e)
                    if more or e == 0:
                        act.wait_ge(s_wolo, d + (e + 2))
                        act.dma_start(wo_raw[:, :], w_out_v[d + e + 1] if isinstance(d, int)
                                      else w_out_v[bass.ds(d + (e + 1), 1)].rearrange("o p c -> (o p) c")).then_inc(wo_in, 16)

                with act.Fori(0, (CT - 2) // 2) as j:
                    d = j * 2
                    for e in range(2):
                        branch_r(d, e, True)
                for e in range(2):
                    branch_r(CT - 2, e, False)
                act.wait_ge(s_wolo, CT + 1)
                act.dma_start(wo_raw[:, :], post_w[0:1, :].to_broadcast([P, D])).then_inc(pw_in, 16)

                def m_hi(t, e):
                    nc.scalar.activation(r1_hi[:, e, :].rearrange("p (k c) -> p k c", c=P),
                                         m_t[:, :, bass.ds(t * P + e * P, P)], ACT.Copy).then_inc(s_mhi, 1)

                def out_stats(t, e):
                    act.wait_ge(s_o, t + (e + 1))
                    nc.scalar.activation(tmp[:, :], pair[e][:, :], ACT.Square,
                                         accum_out=so[:, 0, bass.ds(t + e, 1)]).then_inc(s_oss, 1)
                    act.wait_ge(s_oss, 2 * t + (2 * e + 2))
                    nc.scalar.activation(so[:, 2, bass.ds(t + e, 1)], so[:, 1, bass.ds(t + e, 1)], ACT.Sqrt).then_inc(s_ostd, 1)

                act.wait_ge(s_m, 2 * CT + 2)
                m_hi(0, 0)
                m_hi(0, 1)
                with act.Fori(0, (TT - 2) // 2) as j:
                    t = j * 2
                    for e in range(2):
                        out_stats(t, e)
                        m_hi(t + 2, e)
                for e in range(2):
                    out_stats(TT - 2, e)

            @block.vector
            def _(dve):
                def split_lo(count, e):
                    dve.wait_ge(s_whi, count)
                    nc.vector.tensor_tensor(w_lo[:, e, :, :], raw[:, e, :].rearrange("p (k c) -> p k c", c=P),
                                            w_hi[:, e, :, :].bitcast(f32), ALU.subtract).then_inc(s_wlo, 1)

                for k in range(KT):
                    dve.wait_ge(s_uhi, k + 1)
                    nc.vector.tensor_tensor(r2_lo[:, k, :], r2_lo[:, k, :].bitcast(f32), r2_hi[:, k, :].bitcast(f32),
                                            ALU.subtract).then_inc(s_ulo, 1)
                def split_ur_lo(k):
                    dve.wait_ge(s_urhi, k + 1)
                    nc.vector.tensor_tensor(r1_lo[:, k, :], r1_lo[:, k, :].bitcast(f32), r1_hi[:, k, :].bitcast(f32),
                                            ALU.subtract).then_inc(s_urlo, 1)

                def branch_a(d, e):
                    row = m_t[:, d + e, :] if isinstance(d, int) else m_t[:, bass.ds(d + e, 1), :].rearrange("p o c -> p (o c)")
                    dve.wait_ge(s_full, d + (e + 1))
                    dve.wait_ge(sg_in[e], d * 8 + 16)
                    nc.vector.tensor_tensor(row, pair[e][:, :], two[:, e, :], ALU.mult).then_inc(s_m, 1)
                    split_lo(d + (A0 + e + 3), e)

                for k in range(KT // 2):
                    split_ur_lo(k)
                for e in range(2):
                    branch_a(0, e)
                for k in range(KT // 2, KT):
                    split_ur_lo(k)
                with dve.Fori(1, CT // 2) as j:
                    d = j * 2
                    for e in range(2):
                        branch_a(d, e)

                def branch_r(d, e, more):
                    dve.wait_ge(s_wohi, d + (e + 1))
                    row = lambda z: z[:, bass.ds(d + e, 1), :].rearrange("p o c -> p (o c)")
                    nc.vector.tensor_tensor(row(r2_lo), wo_raw[:, :], row(r2_hi).bitcast(f32), ALU.subtract).then_inc(s_wolo, 1)
                    dve.wait_ge(s_full, d + (CT + e + 1))
                    dve.wait_ge(sg_in[e], d * 8 + (CT * 8 + 16))
                    dve.wait_ge(s_m, d + (CT + e + 2))
                    nc.vector.tensor_tensor(tmp[:, :], pair[e][:, :], two[:, e, :], ALU.mult).then_inc(s_mr, 1)
                    dve.wait_ge(s_mr, d + (e + 1))
                    nc.vector.tensor_tensor(row(m_t), row(m_t), tmp[:, :], ALU.add).then_inc(s_m, 1)
                    if more:
                        split_lo(d + (R0 + e + 3), e)

                with dve.Fori(0, (CT - 2) // 2) as j:
                    d = j * 2
                    for e in range(2):
                        branch_r(d, e, True)
                for e in range(2):
                    branch_r(CT - 2, e, False)

                def m_lo(t, e):
                    dve.wait_ge(s_mhi, t + (e + 1))
                    nc.vector.tensor_tensor(r1_lo[:, e, :].rearrange("p (k c) -> p k c", c=P),
                                            m_t[:, :, bass.ds(t * P + e * P, P)],
                                            r1_hi[:, e, :].rearrange("p (k c) -> p k c", c=P).bitcast(f32),
                                            ALU.subtract).then_inc(s_mlo, 1)

                def finish(t, e):
                    c = lambda k: so[:, k, bass.ds(t + e, 1)]
                    dve.wait_ge(s_oss, 2 * t + (2 * e + 1))
                    nc.vector.tensor_scalar(c(1), c(0), 1.0 / D, EPS, ALU.mult, ALU.add).then_inc(s_oss, 1)
                    dve.wait_ge(s_ostd, t + (e + 1))
                    nc.vector.reciprocal(c(3), c(2)).then_inc(s_orstd, 1)
                    dve.wait_ge(s_orstd, t + (e + 1))
                    dve.wait_ge(s_oout[e], t * 8 + 16)
                    nc.vector.scalar_tensor_tensor(raw[:, e, :], pair[e][:, :], c(3), wo_raw[:, :],
                                                   ALU.mult, ALU.mult).then_inc(s_onorm, 1)
                    dve.wait_ge(s_onorm, t + (e + 3))
                    dve.wait_ge(x_in[e], t * 8 + 16)
                    nc.vector.tensor_tensor(raw[:, e, :], raw[:, e, :], two[:, e, :], ALU.add).then_inc(s_oadd, 1)

                dve.wait_ge(s_m, 2 * CT + 2)
                m_lo(0, 0)
                m_lo(0, 1)
                dve.wait_ge(pw_in, 16)
                with dve.Fori(0, (TT - 2) // 2) as j:
                    t = j * 2
                    for e in range(2):
                        finish(t, e)
                        m_lo(t + 2, e)
                for e in range(2):
                    finish(TT - 2, e)

            @block.tensor
            def _(pe):
                def rank(e, kt, hi, lo):
                    for part in range(6):
                        w = (w_hi if part < 4 else w_lo)[:, e, kt, :]
                        u = lo if part in (2, 3) else hi
                        cols = slice((part % 2) * BANK, (part % 2 + 1) * BANK)
                        last = nc.tensor.matmul(pair[e][:, cols], w, u[:, kt, cols],
                                                start=(kt == 0 and part < 2), stop=(kt == KT - 1 and part >= 4))
                    return last

                def branch(d, e, n, hi, lo):
                    pe.wait_ge(s_whi, d + ((A0, R0)[n] + e + 1))
                    pe.wait_ge(s_wlo, d + ((A0, R0)[n] + e + 3))
                    pe.wait_ge(s_m, d + (n * CT + e + 1))
                    for kt in range(KT):
                        last = rank(e, kt, hi, lo)
                    last.then_inc(s_full, 1)

                for e in range(2):
                    pe.wait_ge(s_whi, A0 + e + 1)
                    pe.wait_ge(s_wlo, A0 + e + 3)
                for kt in range(KT):
                    pe.wait_ge(s_ulo, kt + 1)
                    for e in range(2):
                        last = rank(e, kt, r2_hi, r2_lo)
                        if kt == KT - 1:
                            last.then_inc(s_full, 1)
                with pe.Fori(1, CT // 2) as j:
                    d = j * 2
                    for e in range(2):
                        branch(d, e, 0, r2_hi, r2_lo)
                pe.wait_ge(s_urlo, KT)
                with pe.Fori(0, CT // 2) as j:
                    d = j * 2
                    for e in range(2):
                        branch(d, e, 1, r1_hi, r1_lo)
                pe.wait_ge(s_wolo, CT + 1)
                with pe.Fori(0, TT // 2) as j:
                    t = j * 2
                    for e in range(2):
                        pe.wait_ge(s_mlo, t + (e + 1))
                        pe.wait_ge(s_onorm, t + (e + 1))
                        for kt in range(KT):
                            for part in range(6):
                                m = (r1_hi if part < 4 else r1_lo)[:, e, kt * P:(kt + 1) * P]
                                w = r2_lo if part in (2, 3) else r2_hi
                                cols = slice((part % 2) * BANK, (part % 2 + 1) * BANK)
                                last = nc.tensor.matmul(pair[e][:, cols], m, w[:, kt, cols],
                                                        start=(kt == 0 and part < 2), stop=(kt == KT - 1 and part >= 4))
                        last.then_inc(s_o, 1)


_INS = ["x", "pre_norm_w", "w_in", "b_in", "conv_w", "conv_b", "rg_wa", "rg_ba", "rg_wx", "rg_bx",
        "rg_lambda", "w_branch_a", "w_branch_r", "w_out", "post_norm_w"]


def kernel(**inputs):
    import numpy as _np
    import concourse.bacc as _bacc
    from concourse import mybir as _mybir
    from concourse.bass_utils import run_bass_kernel_spmd as _run

    nc = _bacc.Bacc("TRN2", target_bir_lowering=False, num_devices=1)
    arrays, args = {}, []
    for name in _INS:
        a = _np.ascontiguousarray(inputs[name])
        arrays[f"in_{name}"] = a
        args.append(nc.dram_tensor(f"in_{name}", a.shape, _mybir.dt.from_np(a.dtype), kind="ExternalInput").ap())
    args.append(nc.dram_tensor("out_0", (1, SEQ, D), _mybir.dt.float32, kind="ExternalOutput").ap())
    build(nc, *args)
    r = _run(nc, [arrays], core_ids=[0])
    return r.results[0]["out_0"]
```
